# Optimizing a Trainium2 kernel written in Bass

```python
import jax, jax.numpy as jnp
from jax import lax
import numpy as np
import math

D_MODEL = 1024
BATCH = 1
SEQ = 256
DEPTH = 2

N_RET_HEADS = 4
RET_HEAD_DIM = 128
RET_WIDTH = N_RET_HEADS * RET_HEAD_DIM
POOL_WINDOWS = (2, 4, 8, 16)
POOL_GROUP_DIM = 128
POOL_WIDTH = len(POOL_WINDOWS) * POOL_GROUP_DIM
MIX_WIDTH = RET_WIDTH + POOL_WIDTH
IN_WIDTH = 4 * RET_WIDTH + POOL_WIDTH
CHUNK = 128
ROPE_BASE = 10000.0
CONV_WIDTH = 31
D_FF = -(-8 * D_MODEL // (3 * 256)) * 256
EPS = 1e-6
N_EVEN = (DEPTH + 1) // 2
N_ODD = DEPTH // 2


def rms_norm(x, g):
    x32 = x.astype(jnp.float32)
    y = x32 * lax.rsqrt(jnp.mean(x32 * x32, axis=-1, keepdims=True) + EPS)
    return (y * g).astype(x.dtype)

def rope(t, positions):
    half = t.shape[-1] // 2
    inv_freq = ROPE_BASE ** (-jnp.arange(half, dtype=jnp.float32) / half)
    ang = positions.astype(jnp.float32)[..., None] * inv_freq
    cos = jnp.cos(ang)[:, :, None, :]
    sin = jnp.sin(ang)[:, :, None, :]
    t1, t2 = t[..., :half], t[..., half:]
    return jnp.concatenate([t1 * cos - t2 * sin, t1 * sin + t2 * cos], axis=-1)

def retention(q, k, v, positions):
    B, S, H, Dh = q.shape
    n_chunks = S // CHUNK
    q = rope(q, positions)
    k = rope(k, positions) * (Dh ** -0.5)
    log_gamma = jnp.log1p(-(2.0 ** (-5.0 - jnp.arange(H, dtype=jnp.float32))))
    idx = jnp.arange(CHUNK, dtype=jnp.float32)
    rel = idx[:, None] - idx[None, :]
    decay_mask = jnp.where(rel >= 0, jnp.exp(log_gamma[:, None, None] * jnp.maximum(rel, 0.0)), 0.0)
    q_decay = jnp.exp(log_gamma[:, None] * (idx + 1.0))
    k_decay = jnp.exp(log_gamma[:, None] * (CHUNK - 1.0 - idx))
    chunk_decay = jnp.exp(log_gamma * CHUNK)

    def to_chunks(t):
        return t.reshape(B, n_chunks, CHUNK, H, Dh).transpose(0, 3, 1, 2, 4)

    qc, kc, vc = to_chunks(q), to_chunks(k), to_chunks(v)
    scores = jnp.einsum('bhncd,bhnmd->bhncm', qc, kc) * decay_mask[:, None]
    o_intra = jnp.einsum('bhncm,bhnme->bhnce', scores, vc)
    kv = jnp.einsum('bhnmd,bhnme->nbhde', kc * k_decay[:, None, :, None], vc)

    def step(state, kv_n):
        return state * chunk_decay[None, :, None, None] + kv_n, state

    _, prev_states = lax.scan(step, jnp.zeros((B, H, Dh, Dh), jnp.float32), kv)
    o_cross = jnp.einsum('bhncd,nbhde->bhnce', qc * q_decay[:, None, :, None], prev_states)
    return (o_intra + o_cross).transpose(0, 2, 3, 1, 4).reshape(B, S, H, Dh)

def multiscale_pool(u, pool_w, pool_scale):
    B, S, _ = u.shape
    u32 = u.astype(jnp.float32)
    cs0 = jnp.pad(jnp.cumsum(u32, axis=1), ((0, 0), (1, 0), (0, 0)))
    t = jnp.arange(S)
    outs = []
    for gi, w in enumerate(POOL_WINDOWS):
        c = cs0[:, :, gi * POOL_GROUP_DIM:(gi + 1) * POOL_GROUP_DIM]
        lower = jnp.pad(c[:, :S + 1 - w], ((0, 0), (w - 1, 0), (0, 0)))
        count = jnp.minimum(t + 1, w).astype(jnp.float32)[None, :, None]
        y = (c[:, 1:] - lower) / count - u32[:, :, gi * POOL_GROUP_DIM:(gi + 1) * POOL_GROUP_DIM]
        outs.append(jnp.einsum('bsc,cd->bsd', y.astype(u.dtype), pool_w[gi]))
    return jnp.concatenate(outs, axis=-1) * pool_scale

def retention_pool_mixer(h, positions, w_in, ret_norm_g, pool_w, pool_scale, w_out):
    B, S, _ = h.shape
    proj = h @ w_in
    q, k, v, g, u = jnp.split(proj, [RET_WIDTH, 2 * RET_WIDTH, 3 * RET_WIDTH, 4 * RET_WIDTH], axis=-1)

    def heads(t):
        return t.reshape(B, S, N_RET_HEADS, RET_HEAD_DIM).astype(jnp.float32)

    o = retention(heads(q), heads(k), heads(v), positions)
    mu = jnp.mean(o, axis=-1, keepdims=True)
    var = jnp.mean(jnp.square(o - mu), axis=-1, keepdims=True)
    o = ((o - mu) * lax.rsqrt(var + EPS)).reshape(B, S, RET_WIDTH) * ret_norm_g
    ret_out = (jax.nn.silu(g.astype(jnp.float32)) * o).astype(h.dtype)
    pool_out = multiscale_pool(u, pool_w, pool_scale).astype(h.dtype)
    return jnp.concatenate([ret_out, pool_out], axis=-1) @ w_out

def conformer_conv(h, w_pw1, b_pw1, w_dw, b_dw, ln_g, ln_b, w_pw2, b_pw2):
    a, gate = jnp.split(h @ w_pw1 + b_pw1, 2, axis=-1)
    u = a * jax.nn.sigmoid(gate)
    dw = lax.conv_general_dilated(
        u, w_dw[:, None, :], window_strides=(1,), padding=((CONV_WIDTH - 1, 0),),
        dimension_numbers=('NWC', 'WIO', 'NWC'), feature_group_count=D_MODEL) + b_dw
    d32 = dw.astype(jnp.float32)
    mu = jnp.mean(d32, axis=-1, keepdims=True)
    var = jnp.mean(jnp.square(d32 - mu), axis=-1, keepdims=True)
    z = (d32 - mu) * lax.rsqrt(var + EPS) * ln_g + ln_b
    z = jax.nn.silu(z).astype(h.dtype)
    return z @ w_pw2 + b_pw2

def swiglu(h, w_gate, w_up, w_down):
    return (jax.nn.silu(h @ w_gate) * (h @ w_up)) @ w_down

def first_inputs(seed: int = 0) -> dict:
    key = jax.random.key(seed)
    ks = jax.random.split(key, 24)
    f32 = jnp.float32

    def dense(k, shape, fan_in):
        return jax.random.normal(k, shape, f32) * (fan_in ** -0.5)

    def gain(k, shape):
        return 1.0 + 0.05 * jax.random.normal(k, shape, f32)

    def bias(k, shape):
        return 0.01 * jax.random.normal(k, shape, f32)

    return {
        "x": jax.random.normal(ks[0], (BATCH, SEQ, D_MODEL), f32),
        "positions": jnp.broadcast_to(jnp.arange(SEQ, dtype=jnp.int32), (BATCH, SEQ)),
        "mixer_norm_g": gain(ks[1], (DEPTH, D_MODEL)),
        "ffn_norm_g": gain(ks[2], (DEPTH, D_MODEL)),
        "final_norm_g": gain(ks[3], (D_MODEL,)),
        "ret_w_in": dense(ks[4], (N_EVEN, D_MODEL, IN_WIDTH), D_MODEL),
        "ret_norm_g": gain(ks[5], (N_EVEN, RET_WIDTH)),
        "pool_w": dense(ks[6], (N_EVEN, len(POOL_WINDOWS), POOL_GROUP_DIM, POOL_GROUP_DIM), POOL_GROUP_DIM),
        "pool_scale": gain(ks[7], (N_EVEN, POOL_WIDTH)),
        "mix_w_out": dense(ks[8], (N_EVEN, MIX_WIDTH, D_MODEL), MIX_WIDTH),
        "conv_w_pw1": dense(ks[9], (N_ODD, D_MODEL, 2 * D_MODEL), D_MODEL),
        "conv_b_pw1": bias(ks[10], (N_ODD, 2 * D_MODEL)),
        "conv_w_dw": dense(ks[11], (N_ODD, CONV_WIDTH, D_MODEL), CONV_WIDTH),
        "conv_b_dw": bias(ks[12], (N_ODD, D_MODEL)),
        "conv_ln_g": gain(ks[13], (N_ODD, D_MODEL)),
        "conv_ln_b": bias(ks[14], (N_ODD, D_MODEL)),
        "conv_w_pw2": dense(ks[15], (N_ODD, D_MODEL, D_MODEL), D_MODEL),
        "conv_b_pw2": bias(ks[16], (N_ODD, D_MODEL)),
        "ffn_w_gate": dense(ks[17], (DEPTH, D_MODEL, D_FF), D_MODEL),
        "ffn_w_up": dense(ks[18], (DEPTH, D_MODEL, D_FF), D_MODEL),
        "ffn_w_down": dense(ks[19], (DEPTH, D_FF, D_MODEL), D_FF),
    }

def first_block(x, positions, mixer_norm_g, ffn_norm_g, final_norm_g, ret_w_in, ret_norm_g,
              pool_w, pool_scale, mix_w_out, conv_w_pw1, conv_b_pw1, conv_w_dw, conv_b_dw,
              conv_ln_g, conv_ln_b, conv_w_pw2, conv_b_pw2, ffn_w_gate, ffn_w_up, ffn_w_down):
    h = x
    for layer in range(DEPTH):
        i = layer // 2
        hn = rms_norm(h, mixer_norm_g[layer])
        if layer % 2 == 0:
            h = h + retention_pool_mixer(hn, positions, ret_w_in[i], ret_norm_g[i],
                                         pool_w[i], pool_scale[i], mix_w_out[i])
        else:
            h = h + conformer_conv(hn, conv_w_pw1[i], conv_b_pw1[i], conv_w_dw[i], conv_b_dw[i],
                                   conv_ln_g[i], conv_ln_b[i], conv_w_pw2[i], conv_b_pw2[i])
        h = h + swiglu(rms_norm(h, ffn_norm_g[layer]), ffn_w_gate[layer], ffn_w_up[layer], ffn_w_down[layer])
    return rms_norm(h, final_norm_g)


N_MIXERS = 2
CONV_WIDTH_2 = 3
HEAD_DIM = 64
N_Q_HEADS = D_MODEL // HEAD_DIM
N_KV_HEADS = 4
GROUP = N_Q_HEADS // N_KV_HEADS
WINDOW = 128
BLOCK = 128
D_FF_2 = ((8 * D_MODEL // 3 + 255) // 256) * 256
QKV_WIDTH = (N_Q_HEADS + 2 * N_KV_HEADS) * HEAD_DIM
N_CONV_LAYERS = (DEPTH + 1) // 2
N_ATTN_LAYERS = DEPTH // 2


def rmsnorm(x, gain):
    xf = x.astype(jnp.float32)
    r = lax.rsqrt(jnp.mean(xf * xf, axis=-1, keepdims=True) + EPS)
    return (xf * r).astype(x.dtype) * gain

def alibi_slopes():
    h = jnp.arange(1, N_Q_HEADS + 1, dtype=jnp.float32)
    return jnp.exp2(-8.0 * h / N_Q_HEADS)

def short_conv_mixer(h, w_in, conv_w, w_out):
    d = h.shape[-1]
    bcx = h @ w_in
    b_gate, c_gate, xv = jnp.split(bcx, 3, axis=-1)
    u = b_gate * xv
    y = lax.conv_general_dilated(
        u, conv_w[:, None, :].astype(u.dtype),
        window_strides=(1,), padding=[(CONV_WIDTH_2 - 1, 0)],
        dimension_numbers=('NWC', 'WIO', 'NWC'), feature_group_count=d)
    return (c_gate * y) @ w_out

def swa_sink_attention(h, w_qkv, q_gain, k_gain, sinks, w_o):
    bsz, s, _ = h.shape
    nb = s // BLOCK
    qkv = h @ w_qkv
    q_end = N_Q_HEADS * HEAD_DIM
    k_end = q_end + N_KV_HEADS * HEAD_DIM
    q = qkv[..., :q_end].reshape(bsz, s, N_KV_HEADS, GROUP, HEAD_DIM)
    k = qkv[..., q_end:k_end].reshape(bsz, s, N_KV_HEADS, HEAD_DIM)
    v = qkv[..., k_end:].reshape(bsz, s, N_KV_HEADS, HEAD_DIM)
    q = rmsnorm(q, q_gain)
    k = rmsnorm(k, k_gain)

    qb = q.reshape(bsz, nb, BLOCK, N_KV_HEADS, GROUP, HEAD_DIM)

    def band(t):
        tp = jnp.pad(t, ((0, 0), (BLOCK, 0), (0, 0), (0, 0)))
        tb = tp.reshape(bsz, nb + 1, BLOCK, N_KV_HEADS, HEAD_DIM)
        return jnp.concatenate([tb[:, :-1], tb[:, 1:]], axis=2)

    kw = band(k)
    vw = band(v)

    scale = 1.0 / math.sqrt(HEAD_DIM)
    scores = jnp.einsum('bnqkgd,bnskd->bnkgqs', qb, kw).astype(jnp.float32) * scale

    qi = jnp.arange(BLOCK)[:, None]
    kj = jnp.arange(2 * BLOCK)[None, :]
    dist = qi + BLOCK - kj
    key_pos = (jnp.arange(nb) * BLOCK - BLOCK)[:, None, None] + kj[None]
    mask = (dist >= 0)[None] & (dist < WINDOW)[None] & (key_pos >= 0)

    slopes = alibi_slopes().reshape(N_KV_HEADS, GROUP)
    alibi = -slopes[:, :, None, None] * dist.astype(jnp.float32)[None, None]
    scores = scores + alibi[None, None]
    scores = jnp.where(mask[None, :, None, None], scores, -jnp.inf)

    sink = sinks.astype(jnp.float32).reshape(N_KV_HEADS, GROUP)
    sink_col = jnp.broadcast_to(sink[None, None, :, :, None, None],
                                scores.shape[:-1] + (1,))
    logits = jnp.concatenate([scores, sink_col], axis=-1)
    p = jax.nn.softmax(logits, axis=-1)[..., :-1]

    out = jnp.einsum('bnkgqs,bnskd->bnqkgd', p.astype(vw.dtype), vw)
    out = out.reshape(bsz, s, N_Q_HEADS * HEAD_DIM)
    return out @ w_o

def swiglu_ffn(h, w_gate_up, w_down):
    gu = h @ w_gate_up
    g, u = jnp.split(gu, 2, axis=-1)
    return (jax.nn.silu(g) * u) @ w_down

def second_inputs(seed: int = 0) -> dict:
    key = jax.random.key(seed)
    ks = jax.random.split(key, 14)
    f32 = jnp.float32
    d = D_MODEL

    def w(k, shape, fan_in):
        return jax.random.normal(k, shape, f32) * (fan_in ** -0.5)

    return {
        "x": jax.random.normal(ks[0], (BATCH, SEQ, d), f32),
        "conv_w_in": w(ks[1], (N_CONV_LAYERS, d, 3 * d), d),
        "conv_w": w(ks[2], (N_CONV_LAYERS, CONV_WIDTH_2, d), CONV_WIDTH_2),
        "conv_w_out": w(ks[3], (N_CONV_LAYERS, d, d), d),
        "attn_w_qkv": w(ks[4], (N_ATTN_LAYERS, d, QKV_WIDTH), d),
        "attn_q_gain": 1.0 + 0.05 * jax.random.normal(ks[5], (N_ATTN_LAYERS, HEAD_DIM), f32),
        "attn_k_gain": 1.0 + 0.05 * jax.random.normal(ks[6], (N_ATTN_LAYERS, HEAD_DIM), f32),
        "attn_sinks": 0.5 * jax.random.normal(ks[7], (N_ATTN_LAYERS, N_Q_HEADS), f32),
        "attn_w_o": w(ks[8], (N_ATTN_LAYERS, N_Q_HEADS * HEAD_DIM, d), N_Q_HEADS * HEAD_DIM),
        "norm_mixer": 1.0 + 0.05 * jax.random.normal(ks[9], (DEPTH, d), f32),
        "norm_ffn": 1.0 + 0.05 * jax.random.normal(ks[10], (DEPTH, d), f32),
        "ffn_w_gate_up": w(ks[11], (DEPTH, d, 2 * D_FF_2), d),
        "ffn_w_down": w(ks[12], (DEPTH, D_FF_2, d), D_FF_2),
    }

def second_block(x, conv_w_in, conv_w, conv_w_out, attn_w_qkv, attn_q_gain, attn_k_gain,
              attn_sinks, attn_w_o, norm_mixer, norm_ffn, ffn_w_gate_up, ffn_w_down):
    for i in range(DEPTH):
        h = rmsnorm(x, norm_mixer[i])
        j = i // N_MIXERS
        if i % N_MIXERS == 0:
            mix = short_conv_mixer(h, conv_w_in[j], conv_w[j], conv_w_out[j])
        else:
            mix = swa_sink_attention(h, attn_w_qkv[j], attn_q_gain[j], attn_k_gain[j],
                                     attn_sinks[j], attn_w_o[j])
        x = x + mix
        h = rmsnorm(x, norm_ffn[i])
        x = x + swiglu_ffn(h, ffn_w_gate_up[i], ffn_w_down[i])
    return x


def setup_inputs(seed=0):
    out = dict(first_inputs(seed))
    for name, value in second_inputs(seed + 1).items():
        if name != "x":
            out[name + "_2"] = value
    return out


def reference(
    x, positions, mixer_norm_g, ffn_norm_g, final_norm_g, ret_w_in, ret_norm_g, pool_w,
    pool_scale, mix_w_out, conv_w_pw1, conv_b_pw1, conv_w_dw, conv_b_dw, conv_ln_g, conv_ln_b,
    conv_w_pw2, conv_b_pw2, ffn_w_gate, ffn_w_up, ffn_w_down, conv_w_in_2, conv_w_2,
    conv_w_out_2, attn_w_qkv_2, attn_q_gain_2, attn_k_gain_2, attn_sinks_2, attn_w_o_2,
    norm_mixer_2, norm_ffn_2, ffn_w_gate_up_2, ffn_w_down_2,
):
    x = first_block(
        x, positions, mixer_norm_g, ffn_norm_g, final_norm_g, ret_w_in, ret_norm_g, pool_w,
        pool_scale, mix_w_out, conv_w_pw1, conv_b_pw1, conv_w_dw, conv_b_dw, conv_ln_g,
        conv_ln_b, conv_w_pw2, conv_b_pw2, ffn_w_gate, ffn_w_up, ffn_w_down,
    )
    return second_block(
        x, conv_w_in_2, conv_w_2, conv_w_out_2, attn_w_qkv_2, attn_q_gain_2, attn_k_gain_2,
        attn_sinks_2, attn_w_o_2, norm_mixer_2, norm_ffn_2, ffn_w_gate_up_2, ffn_w_down_2,
    )


_drawn_inputs = setup_inputs


def setup_inputs(seed=0):
    import zlib

    import numpy as np

    out = dict(_drawn_inputs(seed))
    spreads = {}
    factors = {'conv_b_pw1': 7.315,
     'conv_b_dw': 3.604,
     'conv_ln_b': 7.818,
     'conv_b_pw2': 4.713,
     'attn_q_gain_2': 5.508,
     'attn_k_gain_2': 7.588,
     'attn_sinks_2': 74.83}
    for name, (base, spread) in spreads.items():
        noise = np.random.default_rng([zlib.crc32(name.encode()), seed]).standard_normal(out[name].shape)
        drawn = base * np.exp(spread * noise) if base else spread * noise
        out[name] = __import__('jax').numpy.asarray(drawn.astype(out[name].dtype))
    for name, factor in factors.items():
        out[name] = (out[name] * factor).astype(out[name].dtype)
    return out
```

```python
from contextlib import ExitStack

import numpy as np
import concourse.bass as bass
from concourse import mybir

F32 = mybir.dt.float32
F32R = mybir.dt.float32r
I32 = mybir.dt.int32
ALU = mybir.AluOpType
ACT = mybir.ActivationFunctionType
AX = mybir.AxisListType

P = 128
D = 1024
T = 256
KD = D // P
FF = 2816
KF = FF // P
EPS = 1e-6
PIECE = 1024
CHUNK = 2 * PIECE
RAW = 3
RING = 6

COLS = {}
_at = 0
for _name, _n in (("mix_g", 16), ("ffn_g", 16), ("fin_g", 8), ("ret_g", 4), ("pool_s", 4), ("b_pw1", 16),
                  ("w_dw", 31 * 8), ("b_dw", 8), ("ln_g", 8), ("ln_b", 8), ("b_pw2", 8), ("w_c3", 24),
                  ("mix2_g", 16), ("ffn2_g", 16)):
    COLS[_name] = _at
    _at += _n
NCOL = _at
C_ID, C_DEC, C_NEG, C_COR, C_INV, C_SGN, C_DG = 0, 128, 128 + 1024, 1408, 1472, 1473, 1474
NCONST = 1474
QG, KG, SK, NROW = 0, 64, 128, 144

TWO_PI = 2.0 * np.pi
P1 = 6.28125
P2 = float(np.float32(np.round((TWO_PI - P1) * 2.0**17) / 2.0**17))
P3 = float(np.float32(np.round((TWO_PI - P1 - P2) * 2.0**27) / 2.0**27))
P4 = float(np.float32(TWO_PI - P1 - P2 - P3))
MAGIC = 1.5 * 2.0**23
HALF_PI = float(np.float32(np.pi / 2))
PI_IN = 3.1415925


class Queue:

    def __init__(self, sem):
        self.sem, self.n, self.items, self.seen = sem, 0, [], {}

    def wait(self, *toks):
        for sem, val in toks:
            if self.seen.get(id(sem), 0) < val:
                self.seen[id(sem)] = val
                self.items.append(lambda e, s=sem, v=val: e.wait_ge(s, v))

    def op(self, fn, *toks):
        self.wait(*toks)
        self.n += 1
        self.items.append(lambda e: fn(e).then_inc(self.sem, 1))
        return (self.sem, self.n)

    def raw(self, fn, *toks):
        self.wait(*toks)
        self.items.append(lambda e: fn(e))

    def play(self, e):
        for item in self.items:
            item(e)


class Slots:

    def __init__(self, aps):
        self.aps, self.free, self.i = aps, [[] for _ in aps], -1

    def next(self):
        self.i += 1
        k = self.i % len(self.aps)
        return k, self.aps[k], self.free[k]


def stretch(ap, axis, n):
    shape = list(ap.shape)
    shape.insert(axis, n)
    return ap.unsqueeze(axis).broadcast_to(shape)


def model_kernel(nc, w, poolw, xT, pos, cols, rows, consts, out):
    ctx = ExitStack()
    with ctx:
        def sb(name, shape, dt=F32):
            return ctx.enter_context(nc.sbuf_tensor(name, shape, dt))

        def sem(name):
            return ctx.enter_context(nc.semaphore(name))

        raw_t = sb("raw_t", [P, RAW, CHUNK])
        hi_t = sb("hi_t", [P, RING, PIECE], F32R)
        lo_t = sb("lo_t", [P, RING, PIECE], F32R)
        h = sb("h", [P, KD, T])
        xh = sb("xh", [P, KD, T], F32R)
        xl = sb("xl", [P, KD, T], F32R)
        fh = sb("fh", [P, KF, T], F32R)
        fl = sb("fl", [P, KF, T], F32R)
        cst = sb("cst", [P, NCONST])
        col = sb("col", [P, NCOL])
        row = sb("row", [P, NROW])
        pw = sb("pw", [P, 4, P])
        one = sb("one", [P, P])
        mh = sb("mh", [P, 32])
        rbc = sb("rbc", [P, T])
        rb2 = sb("rb2", [P, T])
        ssum = sb("ssum", [P, T])
        sq = sb("sq", [P, 2, T])
        dg = sb("dg", [P, 2, P])
        st = sb("st", [P, 2, 2])
        scr = sb("scr", [P, 11776])
        banks = ctx.enter_context(nc.psum_tensor("banks", [P, 8, 512], F32))
        ident = cst[:, C_ID:C_ID + P]

        pe = Queue(sem("s_pe"))
        dve = Queue(sem("s_dve"))
        act = Queue(sem("s_act"))
        pool = Queue(sem("s_pool"))
        sp = Queue(sem("s_sp"))
        s_raw = [sem(f"s_raw{i}") for i in range(RAW)]
        s_ld = {n: sem("s_ld_" + n) for n in ("x", "cst", "col", "row", "pw", "pos")}
        s_out = sem("s_out")

        def colv(name, i):
            return col[:, COLS[name] + i:COLS[name] + i + 1]

        def load(q, name, dst, src):
            q.raw(lambda e: e.dma_start(dst, src).then_inc(s_ld[name], 16))
            return (s_ld[name], 16)

        x_in = load(sp, "x", h[:, :, :], xT)
        cst_in = load(act, "cst", cst[:, :], consts)
        col_in = load(act, "col", col[:, :], cols)
        row_in = load(act, "row", row[:, :], rows)
        posi = scr[:, 0:T].bitcast(I32)
        pos_in = load(act, "pos", posi, pos)
        pw_in = load(act, "pw", pw[:, :, :], poolw)

        n_pieces = w.shape[0] * 2
        hi_tok, lo_tok, freed = {}, {}, {}

        def load_chunk(c):
            if c >= w.shape[0]:
                return
            if c >= RAW:
                for p in (2 * (c - RAW), 2 * (c - RAW) + 1):
                    sp.wait(hi_tok[p], lo_tok[p])
            sp.raw(lambda e: e.dma_start(raw_t[:, c % RAW, :], w[c]).then_inc(s_raw[c % RAW], 16))

        def split(p):
            if p >= n_pieces:
                return
            c, r = p // 2, p % RING
            src = raw_t[:, c % RAW, (p % 2) * PIECE:(p % 2 + 1) * PIECE]
            arrived = (s_raw[c % RAW], 16 * (c // RAW + 1))
            slot_free = [freed[p - RING]] if p >= RING else []
            hi_tok[p] = act.op(lambda e: e.activation(hi_t[:, r, :], src, ACT.Copy), arrived, *slot_free)
            lo_tok[p] = dve.op(lambda e: e.tensor_tensor(lo_t[:, r, :], src, hi_t[:, r, :].bitcast(F32), ALU.subtract),
                               arrived, *slot_free, hi_tok[p])
            if p % 2:
                load_chunk(c + RAW)

        class Stream:
            g = 0

            @classmethod
            def take(cls, n):
                p, r = cls.g // 8, cls.g % 8
                cls.g += n
                s = slice(r * P, (r + n) * P)
                return p, hi_t[:, p % RING, s], lo_t[:, p % RING, s], (r + n == 8)

        def release(p, tok):
            freed[p] = tok
            split(p - 1 + RING)

        bank_free = [[] for _ in range(8)]
        bank_i = [0]

        def bank():
            b = bank_i[0] % 8
            bank_i[0] += 1
            pe.wait(*bank_free[b])
            bank_free[b] = []
            return b, banks[:, b, :]

        def mm(out_, l, r_, start, stop, inc=False, toks=(), skip=False):
            fn = lambda e: e.matmul(out_, l, r_, start=start, stop=stop, skip_group_check=skip)
            if inc:
                return pe.op(fn, *toks)
            pe.raw(fn, *toks)

        def mm3(out_, wt, a_hi, a_lo, toks, first, last, stationary_w, end=None):
            p, w_hi, w_lo, ends = wt
            end = ends if end is None else end
            pairs = ((w_hi, a_hi), (w_hi, a_lo), (w_lo, a_hi))
            tok = None
            for i, (a, b) in enumerate(pairs):
                need = (hi_tok[p], toks[0]) if i == 0 else ((toks[1],) if i == 1 else (lo_tok[p],))
                l, r_ = (a, b) if stationary_w else (b, a)
                tok = mm(out_, l, r_, first and i == 0, last and i == 2, inc=(i == 2 and (end or last)), toks=need)
            if end:
                release(p, tok)
            return tok

        def product(nk, units, a_hi, a_lo, a_tok, evac, hooks=None):
            hooks = hooks or {}
            late = []
            ready = not hooks
            for u, n in enumerate(units):
                b, ps = bank()
                for t in range(n):
                    for k in range(nk):
                        wt = Stream.take(1)
                        tok = mm3(ps[:, t * T:(t + 1) * T], wt, a_hi[:, k, :], a_lo[:, k, :], a_tok[k],
                                  k == 0, k == nk - 1, True)
                late.append((u, b, ps, tok))
                if u in hooks:
                    ready = hooks[u]() or ready
                if ready:
                    for item in late:
                        evac(*item)
                    late = []
            assert not late

        ones_tok = dve.op(lambda e: e.memset(one[:, :], 1.0))
        mh_tok = pool.op(lambda e: e.memset(mh[:, :], -0.5))
        x_tok = [None] * KD
        ss = {}

        sqs = Slots([sq[:, 0, :], sq[:, 1, :]])

        def prep(k, gain, gi, src_tok, square=True, use_x=True):
            if use_x:
                a = act.op(lambda e: e.activation(xh[:, k, :], h[:, k, :], ACT.Copy, scale=colv(gain, gi + k)),
                           *src_tok, col_in)
                b = dve.op(lambda e: e.scalar_tensor_tensor(xl[:, k, :], h[:, k, :], colv(gain, gi + k),
                                                            xh[:, k, :].bitcast(F32), ALU.mult, ALU.subtract), a)
                x_tok[k] = (a, b)
            if square:
                i, buf, free = sqs.next()
                if k == 0:
                    ss["t"] = act.op(lambda e: e.activation(ssum[:, :], h[:, 0, :], ACT.Square), *src_tok,
                                     *ss.get("read", []))
                else:
                    s = act.op(lambda e: e.activation(buf, h[:, k, :], ACT.Square), *src_tok, *free)
                    ss["t"] = dve.op(lambda e: e.tensor_tensor(ssum[:, :], ssum[:, :], buf, ALU.add), s, ss["t"])
                    sqs.free[i] = [ss["t"]]

        rs = {"used": [], "st": []}

        def rms_a():
            b, ps = bank()
            for i in range(2):
                tok = mm(ps[:, i:i + 1], ssum[:, i * P:(i + 1) * P], one[:, 0:1], True, True, inc=True,
                         toks=(ss["t"], ones_tok))
            ss["read"] = [tok]
            a = dve.op(lambda e: e.tensor_scalar(st[:, 0, :], ps[:, 0:2], 1.0 / D, EPS, ALU.mult, ALU.add), tok)
            bank_free[b] = [a]
            c = pool.op(lambda e: e.tensor_tensor(st[:, 1, :], st[:, 0, :], mh[:, 0:2], ALU.pow), a, mh_tok,
                        *rs["st"])
            rs["st"] = []
            for i in range(2):
                d = dve.op(lambda e, i=i: e.tensor_scalar(dg[:, i, :], ident, st[:, 1, i:i + 1], None, ALU.mult),
                           c, cst_in)
            rs["dg"], rs["pow"] = d, c

        def rms_b(square=False):
            b, ps = bank()
            tok = mm(ps[:, 0:T], one[:, :], dg[:, :, :].rearrange("p a b -> p (a b)"), True, True, inc=True,
                     toks=(rs["dg"],))
            rs["t"] = dve.op(lambda e: e.tensor_copy(rbc[:, :], ps[:, 0:T]), tok, *rs["used"])
            bank_free[b] = [rs["t"]]
            rs["used"] = []
            if square:
                rs["t"] = dve.op(lambda e: e.tensor_tensor(rb2[:, :], rbc[:, :], rbc[:, :], ALU.mult), rs["t"])

        def rms_hooks(square=False, extra=None):
            def last():
                rms_b(square)
                if extra:
                    extra()
                return True
            return {0: rms_a, 1: last}

        def scratch(off, n):
            return scr[:, off:off + n]

        f_tok = [None] * KF

        def put_f(k, src, toks, n=1):
            a = act.op(lambda e: e.activation(fh[:, k:k + n, :], src, ACT.Copy), *toks)
            b = dve.op(lambda e: e.tensor_tensor(fl[:, k:k + n, :], src, fh[:, k:k + n, :].bitcast(F32),
                                                 ALU.subtract), a)
            for i in range(n):
                f_tok[k + i] = (a, b)
            return b

        def ffn(next_gain, gi, square=True, use_x=True):
            t_ring = Slots([scratch(i * 512, 512) for i in range(3)])
            s_ring = Slots([scratch(1536 + i * T, T) for i in range(2)])
            m_ring = Slots([scratch(2048 + i * T, T) for i in range(2)])

            def up(u, b, ps, tok):
                i, t, free = t_ring.next()
                j, s, sfree = s_ring.next()
                l, m, mfree = m_ring.next()
                tv = t.rearrange("p (a b) -> p a b", a=2)
                a = dve.op(lambda e: e.tensor_tensor(tv, ps.rearrange("p (a b) -> p a b", a=2),
                                                     stretch(rbc[:, :], 1, 2), ALU.mult), tok, rs["t"], *free)
                bank_free[b] = [a]
                rs["used"] = [a]
                c = act.op(lambda e: e.activation(s, t[:, 0:T], ACT.Silu), a, *sfree)
                d = dve.op(lambda e: e.tensor_tensor(m, s, t[:, T:2 * T], ALU.mult), c, *mfree)
                t_ring.free[i] = s_ring.free[j] = [d]
                m_ring.free[l] = [put_f(u, m, (d,))]

            product(KD, [2] * KF, xh, xl, x_tok, up, rms_hooks())

            def down(u, b, ps, tok):
                a = dve.op(lambda e: e.tensor_tensor(h[:, u, :], ps[:, 0:T], h[:, u, :], ALU.add), tok)
                bank_free[b] = [a]
                prep(u, next_gain, gi, (a,), square, use_x)

            product(KF, [1] * KD, fh, fl, f_tok, down)

        def out_product(next_gain, gi, bias=None):
            def down(u, b, ps, tok):
                if bias is None:
                    a = dve.op(lambda e: e.tensor_tensor(h[:, u, :], ps[:, 0:T], h[:, u, :], ALU.add), tok)
                else:
                    a = dve.op(lambda e: e.scalar_tensor_tensor(h[:, u, :], ps[:, 0:T], colv(bias, u), h[:, u, :],
                                                                ALU.add, ALU.add), tok, col_in)
                bank_free[b] = [a]
                prep(u, next_gain, gi, (a,))

            product(KD, [1] * KD, fh, fl, f_tok, down)

        def retention():
            cos, sin = scratch(0, T), scratch(T, T)
            w0, w1 = scratch(2 * T, T), scratch(3 * T, T)
            cosr, sinr = scratch(4 * T, T), scratch(5 * T, T)
            qk = scratch(6 * T, 8 * T).rearrange("p (a b) -> p a b", a=8)
            vt = scratch(14 * T, 4 * T).rearrange("p (a b) -> p a b", a=2)
            gs = scratch(18 * T, 4 * T).rearrange("p (a b) -> p a b", a=4)
            UP = 16 + T
            up = scratch(22 * T, 4 * UP).rearrange("p (a b) -> p a b", a=4)
            o0 = 22 * T + 4 * UP
            ta = Slots([scratch(o0 + i * 512, 512) for i in range(2)])
            tb = Slots([scratch(o0 + 1024 + i * 512, 512) for i in range(2)])
            o1 = o0 + 2048
            sT = scratch(o1, 4 * 384).rearrange("p (a b) -> p a b", a=4)
            o2 = o1 + 4 * 384
            assert o2 <= 11776
            posf = w0
            t = dve.op(lambda e: e.tensor_copy(posf, posi), pos_in)
            ang = w1
            t = dve.op(lambda e: e.tensor_scalar(ang, posf, cst[:, C_INV:C_INV + 1], None, ALU.mult), t, cst_in)
            kk = cosr
            t = dve.op(lambda e: e.tensor_scalar(kk, ang, float(1 / TWO_PI), MAGIC, ALU.mult, ALU.add), t)
            t = dve.op(lambda e: e.tensor_scalar(kk, kk, MAGIC, None, ALU.subtract), t)
            for c in (P1, P2, P3, P4):
                t = dve.op(lambda e, c=c: e.scalar_tensor_tensor(ang, kk, -c, ang, ALU.mult, ALU.add), t)
            t = dve.op(lambda e: e.tensor_scalar(kk, ang, HALF_PI, float(-TWO_PI), ALU.is_gt, ALU.mult), t)
            t2 = dve.op(lambda e: e.scalar_tensor_tensor(w0, ang, HALF_PI, kk, ALU.add, ALU.add), t)
            t = dve.op(lambda e: e.tensor_scalar(w1, ang, PI_IN, -PI_IN, ALU.min, ALU.max), t2)
            t2 = dve.op(lambda e: e.tensor_scalar(w0, w0, PI_IN, -PI_IN, ALU.min, ALU.max), t2)
            sin_t = act.op(lambda e: e.activation(sin, w1, ACT.Sin, scale=cst[:, C_SGN:C_SGN + 1]), t, t2)
            cos_t = act.op(lambda e: e.activation(cos, w0, ACT.Sin), t2)
            pad_t = pool.op(lambda e: e.memset(up[:, :, 0:16], 0.0))
            rr = {}

            def tables():
                a = dve.op(lambda e: e.tensor_tensor(cosr, cos, rbc[:, :], ALU.mult), cos_t, rs["t"])
                rr["t"] = dve.op(lambda e: e.tensor_tensor(sinr, sin, rbc[:, :], ALU.mult), sin_t, a)

            qk_tok = {}

            def two(ap):
                return ap.rearrange("p (a b) -> p a b", a=2)

            def qk_evac(u, b, ps, tok):
                i, a_, afree = ta.next()
                j, b_, bfree = tb.next()
                a = dve.op(lambda e: e.tensor_tensor(two(a_), two(ps), stretch(cosr, 1, 2), ALU.mult),
                           tok, rr["t"], *afree)
                c = dve.op(lambda e: e.tensor_tensor(two(b_)[0:64], two(ps)[64:128],
                                                     stretch(sinr[64:128], 1, 2), ALU.mult), *bfree)
                c2 = dve.op(lambda e: e.tensor_tensor(two(b_)[64:128], two(ps)[0:64],
                                                      stretch(sinr[0:64], 1, 2), ALU.mult))
                bank_free[b] = [c2]
                d = dve.op(lambda e: e.tensor_tensor(qk[:, 2 * u:2 * u + 2, :], two(a_), two(b_), ALU.add), a, c2)
                ta.free[i] = tb.free[j] = [d]
                qk_tok[u] = d

            product(KD, [2] * 4, xh, xl, x_tok, qk_evac, rms_hooks(extra=tables))

            vb = [bank(), bank()]
            for k in range(KD):
                wt = Stream.take(4)
                for i in range(2):
                    vtok = mm3(vb[i][1], wt, xh[:, k, i * P:(i + 1) * P], xl[:, k, i * P:(i + 1) * P], x_tok[k],
                               k == 0, k == KD - 1, False, end=(i == 1 and wt[3]))
            v_tok = []
            for i in range(2):
                a = dve.op(lambda e, i=i: e.tensor_scalar(vt[:, i, :], vb[i][1], st[:, 1, i:i + 1], None, ALU.mult),
                           vtok, rs["pow"])
                bank_free[vb[i][0]] = [a]
                v_tok.append(a)
            rs["st"] = [v_tok[1]]

            u_tok = {}

            def u_evac(u, b, ps, tok):
                a = dve.op(lambda e: e.tensor_tensor(up[:, 2 * u:2 * u + 2, 16:UP], two(ps),
                                                     stretch(rbc[:, :], 1, 2), ALU.mult), tok, rs["t"])
                bank_free[b] = [a]
                u_tok[u] = a

            product(KD, [2, 2], xh, xl, x_tok, u_evac)
            y_tok = []
            y_ap = [cos, sin, cosr, sinr]
            wide = Slots([scratch(o1, UP), scratch(o1 + UP, UP)])
            for gi in range(4):
                cur, t = up[:, gi, :], u_tok[gi // 2]
                n = gi + 1
                for s in range(n):
                    sh = 1 << s
                    i, dst, free = wide.next()
                    lo = 2 * sh - 1
                    t2 = pool.op(lambda e, dst=dst, cur=cur, sh=sh, lo=lo: e.tensor_tensor(
                        dst[:, lo:UP], cur[:, lo:UP], cur[:, lo - sh:UP - sh], ALU.add),
                        t, pad_t, *free)
                    cur, t = dst, t2
                    wide.free[i] = []
                t = pool.op(lambda e, cur=cur, gi=gi: e.tensor_tensor(
                    cur[:, 16:32], cur[:, 16:32], cst[:, C_COR + 16 * gi:C_COR + 16 * gi + 16], ALU.mult), t, cst_in)
                t = dve.op(lambda e, cur=cur, gi=gi: e.scalar_tensor_tensor(
                    y_ap[gi], cur[:, 16:UP], 1.0 / (2 << gi), up[:, gi, 16:UP], ALU.mult, ALU.subtract),
                    t, *qk_tok.values())
                wide.free[wide.i % 2] = [t]
                y_tok.append(t)
            wide_done = y_tok[3]

            gs_tok = {}

            def g_evac(u, b, ps, tok):
                i, a_, afree = ta.next()
                a = dve.op(lambda e: e.tensor_tensor(two(a_), two(ps), stretch(rbc[:, :], 1, 2), ALU.mult),
                           tok, rs["t"], *afree)
                bank_free[b] = [a]
                rs["used"] = [a]
                c = act.op(lambda e: e.activation(gs[:, 2 * u:2 * u + 2, :], two(a_), ACT.Silu), a)
                ta.free[i] = [c]
                gs_tok[u] = c

            product(KD, [2, 2], xh, xl, x_tok, g_evac)

            s_tok = []
            for hd in range(4):
                b, ps = bank()
                mm(ps[:, 0:T], qk[:, 4 + hd, 0:P], qk[:, hd, :], True, True,
                   toks=(qk_tok[hd // 2], qk_tok[2 + hd // 2]))
                tok = mm(ps[:, T:T + P], qk[:, 4 + hd, P:T], qk[:, hd, P:T], True, True, inc=True)
                dec = cst[:, C_DEC + T * hd:C_DEC + T * hd + T]
                a = dve.op(lambda e, hd=hd, ps=ps, dec=dec: e.tensor_tensor(sT[:, hd, 0:T], ps[:, 0:T], dec, ALU.mult),
                           tok, wide_done)
                a = dve.op(lambda e, hd=hd, ps=ps, dec=dec: e.tensor_tensor(sT[:, hd, T:T + P], ps[:, T:T + P],
                                                                            dec[:, 0:P], ALU.mult))
                bank_free[b] = [a]
                s_tok.append(a)
            for half in range(2):
                b, ps = bank()
                for i in range(2):
                    gi = 2 * half + i
                    tok = mm(ps[:, i * T:(i + 1) * T], pw[:, gi, :], y_ap[gi], True, True, inc=True,
                             toks=(pw_in, y_tok[gi]))
                for i in range(2):
                    gi = 2 * half + i
                    a = act.op(lambda e, gi=gi, i=i, ps=ps: e.activation(
                        fh[:, 4 + gi, :], ps[:, i * T:(i + 1) * T], ACT.Copy, scale=colv("pool_s", gi)), tok, col_in)
                for i in range(2):
                    gi = 2 * half + i
                    c = dve.op(lambda e, gi=gi, i=i, ps=ps: e.scalar_tensor_tensor(
                        fl[:, 4 + gi, :], ps[:, i * T:(i + 1) * T], colv("pool_s", gi),
                        fh[:, 4 + gi, :].bitcast(F32), ALU.mult, ALU.subtract), a)
                    f_tok[4 + gi] = (a, c)
                bank_free[b] = [a, c]
            oT = qk[:, 0:4, :]
            o2 = qk[:, 4:8, :]
            o_tok = []
            for pr in range(2):
                b, ps = bank()
                for i in range(2):
                    hd = 2 * pr + i
                    vs = [vt[:, m, hd * P:(hd + 1) * P] for m in range(2)]
                    mm(ps[:, i * T:(i + 1) * T], vs[0], sT[:, hd, 0:T], True, False, toks=(s_tok[hd], v_tok[1]))
                    tok = mm(ps[:, i * T + P:(i + 1) * T], vs[1], sT[:, hd, T:T + P], False, True, inc=True)
                a = dve.op(lambda e, pr=pr, ps=ps: e.tensor_copy(oT[:, 2 * pr:2 * pr + 2, :], two(ps)), tok)
                bank_free[b] = [a]
                o_tok.append(a)
            sq_tok, d_tok = [], []
            for pr in range(2):
                b, ps = bank()
                tok = mm(ps, one[:, :], oT[:, 2 * pr:2 * pr + 2, :], True, True, inc=True, toks=(o_tok[pr],))
                a = dve.op(lambda e, pr=pr, ps=ps: e.scalar_tensor_tensor(
                    oT[:, 2 * pr:2 * pr + 2, :], two(ps), -1.0 / P, oT[:, 2 * pr:2 * pr + 2, :], ALU.mult, ALU.add),
                    tok)
                bank_free[b] = [a]
                d_tok.append(a)
                sq_tok.append(act.op(lambda e, pr=pr, o2=o2: e.activation(o2[:, 2 * pr:2 * pr + 2, :],
                                                                   oT[:, 2 * pr:2 * pr + 2, :], ACT.Square), a))
            b, ps = bank()
            for hd in range(4):
                for i in range(2):
                    tok = mm(ps[:, 2 * hd + i:2 * hd + i + 1], o2[:, hd, i * P:(i + 1) * P], one[:, 0:1], True, True,
                             inc=True, toks=(sq_tok[hd // 2],))
            gst = up[:, 0, 0:16]
            a = dve.op(lambda e, ps=ps: e.tensor_scalar(gst[:, 0:8], ps[:, 0:8], 1.0 / P, EPS, ALU.mult, ALU.add), tok,
                       *y_tok)
            bank_free[b] = [a]
            c = pool.op(lambda e: e.tensor_tensor(gst[:, 8:16], gst[:, 0:8], mh[:, 0:8], ALU.pow), a)
            dgs = sT.rearrange("p a b -> p (a b)")
            for i in range(8):
                dtok = dve.op(lambda e, i=i: e.tensor_scalar(dgs[:, i * P:(i + 1) * P], ident, gst[:, 8 + i:9 + i],
                                                             None, ALU.mult), c, tok)
            for pr in range(2):
                b, ps = bank()
                tok = mm(ps, one[:, :], dgs[:, pr * 512:(pr + 1) * 512], True, True, inc=True, toks=(dtok,))
                a = dve.op(lambda e, pr=pr, ps=ps: e.tensor_tensor(
                    oT[:, 2 * pr:2 * pr + 2, :], two(ps), oT[:, 2 * pr:2 * pr + 2, :], ALU.mult), tok,
                    sq_tok[pr])
                bank_free[b] = [a]
                for i in range(2):
                    hd = 2 * pr + i
                    c = dve.op(lambda e, hd=hd: e.scalar_tensor_tensor(
                        oT[:, hd, :], oT[:, hd, :], colv("ret_g", hd), gs[:, hd, :], ALU.mult, ALU.mult),
                        a, gs_tok[pr])
                    put_f(hd, oT[:, hd, :], (c,))

        def conformer():
            UP = 32 + T
            u_r = Slots([scratch(i * UP, UP) for i in range(2)])
            o0 = 2 * UP
            t_ring = Slots([scratch(o0 + i * 512, 512) for i in range(2)])
            s_ring = Slots([scratch(o0 + 1024 + i * T, T) for i in range(2)])
            o1 = o0 + 1024 + 2 * T
            dw = scratch(o1, 8 * T).rearrange("p (a b) -> p a b", a=8)
            o2 = o1 + 8 * T
            acc2 = [scratch(o2 + i * T, T) for i in range(2)]
            o3 = o2 + 2 * T
            dsq = scratch(o3, 8 * T).rearrange("p (a b) -> p a b", a=8)
            assert o3 + 8 * T <= 11776
            pads = [pool.op(lambda e, i=i: e.memset(u_r.aps[i][:, 0:32], 0.0), f_tok[KF - 1][1]) for i in range(2)]
            dw_tok = [None] * 8

            def evac(u, b, ps, tok):
                i, t, free = t_ring.next()
                j, s, sfree = s_ring.next()
                l, ub, ufree = u_r.next()
                a = dve.op(lambda e: e.tensor_tensor(t.rearrange("p (a b) -> p a b", a=2),
                                                     ps.rearrange("p (a b) -> p a b", a=2),
                                                     stretch(rbc[:, :], 1, 2), ALU.mult), tok, rs["t"], *free)
                bank_free[b] = [a]
                rs["used"] = [a]
                c = act.op(lambda e: e.activation(s, t[:, T:2 * T], ACT.Sigmoid, bias=colv("b_pw1", 8 + u)), a,
                           *sfree)
                d = dve.op(lambda e: e.scalar_tensor_tensor(ub[:, 32:UP], t[:, 0:T], colv("b_pw1", u), s,
                                                            ALU.add, ALU.mult), c, pads[l], *ufree)
                t_ring.free[i] = s_ring.free[j] = [d]
                acc = [dw[:, u, :], acc2[u % 2]]
                ct = [None, None]
                for k in range(31):
                    q = k % 2
                    src = ub[:, 2 + k:2 + k + T]
                    wk = colv("w_dw", 8 * k + u)
                    if k == 0:
                        ct[0] = dve.op(lambda e, src=src, wk=wk: e.tensor_scalar(
                            acc[0], src, wk, colv("b_dw", u), ALU.mult, ALU.add), d)
                    elif k == 1:
                        ct[1] = dve.op(lambda e, src=src, wk=wk: e.tensor_scalar(
                            acc[1], src, wk, None, ALU.mult), d)
                    else:
                        ct[q] = dve.op(lambda e, q=q, src=src, wk=wk: e.scalar_tensor_tensor(
                            acc[q], src, wk, acc[q], ALU.mult, ALU.add), ct[q])
                u_r.free[l] = [ct[0], ct[1]]
                dw_tok[u] = dve.op(lambda e: e.tensor_tensor(acc[0], acc[0], acc[1], ALU.add), ct[0], ct[1])

            product(KD, [2] * KD, xh, xl, x_tok, evac, rms_hooks())
            b, ps = bank()
            for j in range(8):
                tok = mm(ps[:, 0:T], one[:, :], dw[:, j, :], j == 0, j == 7, inc=True, toks=(dw_tok[j],))
            q_tok = []
            for i in range(4):
                a = dve.op(lambda e, i=i, ps=ps: e.scalar_tensor_tensor(
                    dw[:, 2 * i:2 * i + 2, :], stretch(ps[:, 0:T], 1, 2), -1.0 / D, dw[:, 2 * i:2 * i + 2, :],
                    ALU.mult, ALU.add), tok)
                q_tok.append(act.op(lambda e, i=i: e.activation(dsq[:, 2 * i:2 * i + 2, :], dw[:, 2 * i:2 * i + 2, :],
                                                                ACT.Square), a))
            bank_free[b] = [a]
            b, ps = bank()
            for i in range(2):
                for j in range(8):
                    tok = mm(ps[:, i:i + 1], dsq[:, j, i * P:(i + 1) * P], one[:, 0:1], j == 0, j == 7,
                             inc=(j == 7), toks=(q_tok[j // 2],))
            a = dve.op(lambda e, ps=ps: e.tensor_scalar(st[:, 0, :], ps[:, 0:2], 1.0 / D, EPS, ALU.mult, ALU.add), tok)
            bank_free[b] = [a]
            c = pool.op(lambda e: e.tensor_tensor(st[:, 1, :], st[:, 0, :], mh[:, 0:2], ALU.pow), a)
            for i in range(2):
                d = dve.op(lambda e, i=i: e.tensor_scalar(dg[:, i, :], ident, st[:, 1, i:i + 1], None, ALU.mult), c)
            b, ps = bank()
            tok = mm(ps[:, 0:T], one[:, :], dg[:, :, :].rearrange("p a b -> p (a b)"), True, True, inc=True,
                     toks=(d,))
            for i in range(4):
                a = dve.op(lambda e, i=i, ps=ps: e.tensor_tensor(
                    dw[:, 2 * i:2 * i + 2, :], stretch(ps[:, 0:T], 1, 2), dw[:, 2 * i:2 * i + 2, :], ALU.mult), tok,
                    q_tok[i])
                for j in (2 * i, 2 * i + 1):
                    s = act.op(lambda e, j=j: e.activation(dsq[:, j, :], dw[:, j, :], ACT.Silu,
                                                           scale=colv("ln_g", j), bias=colv("ln_b", j)), a)
                    put_f(j, dsq[:, j, :], (s,))
            bank_free[b] = [a]

        def short_conv():
            UP = 8 + T
            u_r = Slots([scratch(i * UP, UP) for i in range(2)])
            o0 = 2 * UP
            tb = Slots([scratch(o0 + i * T, T) for i in range(2)])
            tc = Slots([scratch(o0 + 2 * T + i * T, T) for i in range(2)])
            y_r = Slots([scratch(o0 + 4 * T + i * T, T) for i in range(2)])
            pads = [pool.op(lambda e, i=i: e.memset(u_r.aps[i][:, 0:8], 0.0), f_tok[KF - 1][1]) for i in range(2)]
            y_of = {}

            def evac(u, b, ps, tok):
                j = u // 2
                if u % 2 == 0:
                    i, t, free = tb.next()
                    l, ub, ufree = u_r.next()
                    m, y, yfree = y_r.next()
                    a = dve.op(lambda e, t=t: e.tensor_tensor(t, ps[:, 0:T], rb2[:, :], ALU.mult), tok, rs["t"], *free)
                    c = dve.op(lambda e, t=t: e.tensor_tensor(ub[:, 8:UP], ps[:, T:2 * T], t, ALU.mult), a, pads[l],
                               *ufree)
                    bank_free[b] = [c]
                    tb.free[i] = [c]
                    d = act.op(lambda e, y=y: e.activation(y, ub[:, 6:6 + T], ACT.Copy, scale=colv("w_c3", j)), c,
                               *yfree)
                    d = dve.op(lambda e, y=y: e.scalar_tensor_tensor(y, ub[:, 7:7 + T], colv("w_c3", 8 + j), y,
                                                                ALU.mult, ALU.add), d)
                    d = dve.op(lambda e, y=y: e.scalar_tensor_tensor(y, ub[:, 8:8 + T], colv("w_c3", 16 + j), y,
                                                                ALU.mult, ALU.add), d)
                    u_r.free[l] = [d]
                    y_of[j] = (m, y, d)
                else:
                    m, y, yt = y_of[j]
                    i, t, free = tc.next()
                    a = dve.op(lambda e, t=t: e.tensor_tensor(t, ps[:, 0:T], rbc[:, :], ALU.mult), tok, rs["t"], *free)
                    bank_free[b] = [a]
                    rs["used"] = [a]
                    c = dve.op(lambda e, t=t, y=y: e.tensor_tensor(t, t, y, ALU.mult), a, yt)
                    y_r.free[m] = [c]
                    tc.free[i] = [put_f(j, t, (c,))]

            product(KD, [2, 1] * KD, xh, xl, x_tok, evac, rms_hooks(square=True))

        def attention():
            o = [0]

            def take(n):
                o[0] += n
                return scr[:, o[0] - n:o[0]]

            qn = take(2 * D).rearrange("p (a b) -> p a b", a=2)
            kv = take(1024).rearrange("p (a b) -> p a b", a=2)
            kd = take(1024).rearrange("p (a b) -> p a b", a=2)
            qT = take(8 * T).rearrange("p (a b) -> p a b", a=8)
            kT = take(4 * T).rearrange("p (a b) -> p a b", a=4)
            sc0 = [take(512).rearrange("p (a b) -> p a b", a=4) for _ in range(1)]
            sc1 = [take(1024).rearrange("p (a b) -> p a b", a=4) for _ in range(1)]
            pT = take(1536)
            on = take(512).rearrange("p (a b) -> p a b", a=2)
            g8 = take(64)
            r1 = take(32)
            r2 = take(32)
            nm = take(8)
            den = take(8)
            es = take(8)
            ms_ = take(8)
            assert o[0] <= 11776, o[0]
            start = f_tok[KF - 1][1]
            g8t = dve.op(lambda e: e.tensor_scalar(g8, row[:, QG:QG + 64], 0.125, None, ALU.mult), row_in, start)

            def project():
                bs = [bank(), bank()]
                for k in range(KD):
                    wt = Stream.take(4)
                    for i in range(2):
                        tok = mm3(bs[i][1], wt, xh[:, k, i * P:(i + 1) * P], xl[:, k, i * P:(i + 1) * P], x_tok[k],
                                  k == 0, k == KD - 1, False, end=(i == 1 and wt[3]))
                return bs, tok

            kvb, kv_mm = project()
            rms_a()
            kvt = []
            for i in range(2):
                a = dve.op(lambda e, i=i: e.tensor_scalar(kv[:, i, :], kvb[i][1], st[:, 1, i:i + 1], None, ALU.mult),
                           kv_mm, rs["pow"])
                bank_free[kvb[i][0]] = [a]
                kvt.append(a)

            def head_norm(src, n, tok, r, sqb, gain, gain_t, dst, free=()):
                a = act.op(lambda e: e.activation(sqb, src, ACT.Square), *tok, *free)
                c = dve.op(lambda e: e.tensor_reduce(r[:, 0:n], sqb, AX.X, ALU.add), a)
                d = dve.op(lambda e: e.tensor_scalar(r[:, 0:n], r[:, 0:n], 1.0 / 64, EPS, ALU.mult, ALU.add), c)
                f = pool.op(lambda e: e.tensor_tensor(r[:, n:2 * n], r[:, 0:n], mh[:, 0:n], ALU.pow), d)
                g = dve.op(lambda e: e.tensor_tensor(src, src, stretch(r[:, n:2 * n], 2, 64), ALU.mult), f)
                return dve.op(lambda e: e.tensor_tensor(dst, src, stretch(gain, 1, n), ALU.mult), g, gain_t)

            heads = lambda ap: ap.rearrange("p (a b) -> p a b", b=64)
            ksq = heads(sc1[0].rearrange("p a b -> p (a b)")[:, 0:256])
            kd_t = []
            for i in range(2):
                s = head_norm(heads(kv[:, i, 0:256]), 4, (kvt[i],), r1[:, 8 * i:8 * i + 8], ksq, row[:, KG:KG + 64],
                              row_in, heads(kv[:, i, 0:256]), free=kd_t[-1:])
                for j in range(2):
                    s2 = dve.op(lambda e, i=i, j=j: e.tensor_copy(
                        kd[:, i, :].rearrange("p (g j d) -> p g j d", j=2, d=64)[:, :, j, :],
                        heads(kv[:, i, 0:256])), s)
                kd_t.append(s2)

            q_done = []
            for c in range(2):
                qb, q_mm = project()
                for i in range(2):
                    dst = qn[:, i, c * 512:(c + 1) * 512]
                    a = dve.op(lambda e, i=i, dst=dst, qb=qb: e.tensor_scalar(dst, qb[i][1], st[:, 1, i:i + 1], None,
                                                                             ALU.mult), q_mm)
                    bank_free[qb[i][0]] = [a]
                    qs = heads(sc1[0].rearrange("p a b -> p (a b)")[:, 0:512])
                    s = head_norm(heads(dst), 8, (a,), r2[:, 16 * i:16 * i + 16], qs, g8, g8t, heads(dst),
                                  free=(kd_t + q_done)[-1:])
                    q_done.append(s)
            rs["st"] = [a]

            kT_t = []
            for half in range(2):
                b, ps = bank()
                for g in range(2):
                    for i in range(2):
                        gg = 2 * half + g
                        tok = pe.op(lambda e, g=g, i=i, gg=gg, ps=ps: e.transpose(
                            ps[:, (2 * g + i) * P:(2 * g + i + 1) * P], kd[:, i, gg * P:(gg + 1) * P], ident), *kd_t)
                a = dve.op(lambda e, half=half, ps=ps: e.tensor_copy(
                    kT[:, 2 * half:2 * half + 2, :], ps.rearrange("p (a b) -> p a b", a=2)), tok)
                bank_free[b] = [a]
                kT_t.append(a)
            qT_t = []
            for t in range(4):
                b, ps = bank()
                for g in range(2):
                    for i in range(2):
                        tt = 2 * t + g
                        tok = pe.op(lambda e, g=g, i=i, tt=tt, ps=ps: e.transpose(
                            ps[:, (2 * g + i) * P:(2 * g + i + 1) * P], qn[:, i, tt * P:(tt + 1) * P], ident),
                            q_done[2 * (t // 2) + i])
                a = act.op(lambda e, t=t, ps=ps: e.activation(
                    qT[:, 2 * t:2 * t + 2, :], ps.rearrange("p (a b) -> p a b", a=2), ACT.Copy), tok)
                bank_free[b] = [a]
                qT_t.append(a)

            negd = cst[:, C_NEG:C_NEG + T]
            prev = {"sc": [], "pT": [], "on": [], "small": []}
            for g in range(4):
                s0, s1 = sc0[0], sc1[0]
                near, far = [bank(), bank()], [bank(), bank()]
                for i in range(4):
                    hd, odd, at = 4 * g + i, i % 2, i // 2
                    r = slice(64 * odd, 64 * odd + 64)
                    mm(near[odd][1][:, at * P:(at + 1) * P], qT[r, hd // 2, 0:P], kT[r, g, 0:P], True, True,
                       toks=(qT_t[g], kT_t[g // 2]))
                    tok = mm(far[odd][1][:, at * T:(at + 1) * T], qT[r, hd // 2, P:T], kT[r, g, :], True, True,
                             inc=True)
                for i in range(4):
                    odd, at = i % 2, i // 2
                    slope = float(2.0 ** (-8.0 * (4 * g + i + 1) / 16))
                    n_ps = near[odd][1][:, at * P:(at + 1) * P]
                    f_ps = far[odd][1][:, at * T:(at + 1) * T]
                    a0 = dve.op(lambda e, i=i, slope=slope, n_ps=n_ps, s0=s0: e.scalar_tensor_tensor(
                        s0[:, i, :], negd[:, P:T], slope, n_ps, ALU.mult, ALU.add), tok, *prev["sc"], q_done[3])
                    a1 = dve.op(lambda e, i=i, slope=slope, f_ps=f_ps, s1=s1: e.scalar_tensor_tensor(
                        s1[:, i, :], negd, slope, f_ps, ALU.mult, ALU.add))
                    bank_free[near[odd][0]] = [a0]
                    bank_free[far[odd][0]] = [a1]
                m0 = dve.op(lambda e, s0=s0: e.tensor_reduce(nm[:, 0:4], s0, AX.X, ALU.max), a0, *prev["small"])
                m1 = dve.op(lambda e, s1=s1: e.tensor_reduce(nm[:, 4:8], s1, AX.X, ALU.max), a1)
                sk = stretch(row[:, SK + 4 * g:SK + 4 * g + 4], 1, 2)
                n8 = nm.rearrange("p (a b) -> p a b", a=2)
                m = dve.op(lambda e, sk=sk, n8=n8: e.tensor_tensor(ms_.rearrange("p (a b) -> p a b", a=2), n8, sk, ALU.max),
                           m0, m1, row_in)
                m2 = dve.op(lambda e, sk=sk: e.tensor_tensor(es.rearrange("p (a b) -> p a b", a=2), sk,
                                                      ms_.rearrange("p (a b) -> p a b", a=2), ALU.subtract), m)
                m3 = dve.op(lambda e: e.tensor_scalar(nm, ms_, -1.0, None, ALU.mult), m)
                x = []
                for i in range(4):
                    x.append(act.op(lambda e, i=i, s0=s0: e.activation(s0[:, i, :], s0[:, i, :], ACT.Exp,
                                                                bias=nm[:, i:i + 1], accum_out=den[:, i:i + 1]), m3))
                    x.append(act.op(lambda e, i=i, s1=s1: e.activation(s1[:, i, :], s1[:, i, :], ACT.Exp,
                                                                bias=nm[:, 4 + i:5 + i],
                                                                accum_out=den[:, 4 + i:5 + i])))
                x.append(act.op(lambda e: e.activation(es, es, ACT.Exp), m2))
                dd = dve.op(lambda e: e.tensor_tensor(den, den, es, ALU.add), x[-1])
                dd = dve.op(lambda e: e.reciprocal(den, den), dd)
                pt = []
                for part in range(3):
                    b, ps = bank()
                    for i in range(4):
                        src = s0[:, i, :] if part == 0 else s1[:, i, (part - 1) * P:part * P]
                        tok = pe.op(lambda e, i=i, src=src, ps=ps: e.transpose(ps[:, i * P:(i + 1) * P], src, ident),
                                    x[2 * i + 1])
                    if part == 1:
                        a = act.op(lambda e, ps=ps, part=part: e.activation(pT[:, part * 512:(part + 1) * 512], ps,
                                                                            ACT.Copy), tok, *prev["pT"])
                    else:
                        a = dve.op(lambda e, ps=ps, part=part: e.tensor_copy(pT[:, part * 512:(part + 1) * 512], ps),
                                   tok, *prev["pT"])
                    bank_free[b] = [a]
                    pt.append(a)
                prev["sc"] = [tok]
                b, ps = bank()
                vs = [kv[:, m_, 256 + 64 * g:256 + 64 * g + 64] for m_ in range(2)]
                for i in range(4):
                    ap = [pT[:, k * 512 + i * P:k * 512 + (i + 1) * P] for k in range(3)]
                    mm(ps[:, i * 64:(i + 1) * 64], ap[0], vs[0], True, True, toks=(*pt, *kvt))
                    mm(ps[:, 256 + i * 64:256 + (i + 1) * 64], ap[1], vs[0], True, False)
                    tok = mm(ps[:, 256 + i * 64:256 + (i + 1) * 64], ap[2], vs[1], False, True, inc=True)
                prev["pT"] = [tok]
                a = dve.op(lambda e, ps=ps: e.tensor_tensor(on.rearrange("p a b -> p (a b)").rearrange(
                    "p (a b) -> p a b", b=64), heads(ps), stretch(den, 2, 64), ALU.mult), tok, dd, *prev["on"])
                bank_free[b] = [a]
                prev["small"] = [a]
                b, ps = bank()
                for t in range(2):
                    for i in range(2):
                        tok = pe.op(lambda e, t=t, i=i, ps=ps: e.transpose(
                            ps[:, (2 * t + i) * P:(2 * t + i + 1) * P], on[:, i, t * P:(t + 1) * P], ident), a)
                prev["on"] = [tok]
                c = put_f(2 * g, ps.rearrange("p (a b) -> p a b", a=2), (tok,), n=2)
                bank_free[b] = [c]

        for c in range(RAW):
            load_chunk(c)
        for k in range(KD):
            prep(k, "mix_g", 0, (x_in,))
        for p in range(RING - 1):
            split(p)
        retention()
        out_product("ffn_g", 0)
        ffn("mix_g", 8)
        conformer()
        out_product("ffn_g", 8, bias="b_pw2")
        ffn("mix_g", 0, use_x=False)
        rms_a()
        rms_b()
        sqk = rs["t"]
        for k in range(KD):
            a = dve.op(lambda e, k=k: e.scalar_tensor_tensor(h[:, k, :], h[:, k, :], colv("fin_g", k), rbc[:, :],
                                                             ALU.mult, ALU.mult), sqk, ss["t"])
            rs["used"] = [a]
            prep(k, "mix2_g", 0, (a,))
        short_conv()
        out_product("ffn2_g", 0)
        ffn("mix2_g", 8)
        attention()
        out_product("ffn2_g", 8)
        outs = []

        def last_prep(k, gain, gi, src_tok, square, use_x):
            sp.raw(lambda e: e.dma_start(out[:, k, :], h[:, k, :]).then_inc(s_out, 16), *src_tok)

        prep = last_prep
        ffn("", 0)
        sp.wait((s_out, 16 * KD))
        assert Stream.g == 8 * n_pieces

        block = ctx.enter_context(nc.Block())

        @block.sync
        def _(e):
            sp.play(e)

        @block.gpsimd
        def _(e):
            pool.play(e)

        @block.scalar
        def _(e):
            act.play(e)

        @block.vector
        def _(e):
            dve.play(e)

        @block.tensor
        def _(e):
            pe.play(e)


def kernel(**inputs):
    import numpy as _np
    import concourse.bacc as _bacc
    from concourse import mybir as _mybir
    from concourse.bass_utils import run_bass_kernel_spmd as _run

    a = {k: _np.asarray(v) for k, v in inputs.items()}

    def tiles(w):
        k, n = w.shape
        return w.reshape(k // 128, 128, n // 128, 128).transpose(1, 2, 0, 3)

    def strips(w):
        k, n = w.shape
        return w.reshape(k // 128, 128, n // 512, 512).transpose(1, 2, 0, 3)

    def flat(t):
        return t.reshape(128, -1)

    def mixed(*parts):
        return flat(_np.stack(parts, axis=2))

    w_in = a["ret_w_in"][0]
    c_in = a["conv_w_in_2"][0]
    qkv = a["attn_w_qkv_2"][0]
    pw1 = a["conv_w_pw1"][0]
    gu2 = a["ffn_w_gate_up_2"]

    def ffn(gate, up, down):
        return [mixed(tiles(gate), tiles(up)), flat(tiles(down))]

    parts = [flat(tiles(w_in[:, 0:1024])), flat(strips(w_in[:, 1024:1536])), flat(tiles(w_in[:, 2048:2560])),
             flat(tiles(w_in[:, 1536:2048])), flat(tiles(a["mix_w_out"][0]))]
    parts += ffn(a["ffn_w_gate"][0], a["ffn_w_up"][0], a["ffn_w_down"][0])
    parts += [mixed(tiles(pw1[:, 0:1024]), tiles(pw1[:, 1024:2048])), flat(tiles(a["conv_w_pw2"][0]))]
    parts += ffn(a["ffn_w_gate"][1], a["ffn_w_up"][1], a["ffn_w_down"][1])
    parts += [mixed(tiles(c_in[:, 0:1024]), tiles(c_in[:, 2048:3072]), tiles(c_in[:, 1024:2048])),
              flat(tiles(a["conv_w_out_2"][0]))]
    parts += ffn(gu2[0][:, 0:2816], gu2[0][:, 2816:], a["ffn_w_down_2"][0])
    parts += [flat(strips(qkv[:, 1024:1536])), flat(strips(qkv[:, 0:1024])), flat(tiles(a["attn_w_o_2"][0]))]
    parts += ffn(gu2[1][:, 0:2816], gu2[1][:, 2816:], a["ffn_w_down_2"][1])
    w = _np.concatenate(parts, axis=1)
    w = _np.ascontiguousarray(w.reshape(128, -1, CHUNK).transpose(1, 0, 2))

    def column(v):
        return _np.asarray(v).reshape(-1, 128).T

    cols = _np.ascontiguousarray(_np.concatenate([
        column(a["mixer_norm_g"]), column(a["ffn_norm_g"]), column(a["final_norm_g"]), column(a["ret_norm_g"]),
        column(a["pool_scale"]), column(a["conv_b_pw1"]), column(a["conv_w_dw"][0]), column(a["conv_b_dw"]),
        column(a["conv_ln_g"]), column(a["conv_ln_b"]), column(a["conv_b_pw2"]), column(a["conv_w_2"][0]),
        column(a["norm_mixer_2"]), column(a["norm_ffn_2"])], axis=1))
    rows = _np.ascontiguousarray(_np.broadcast_to(_np.concatenate(
        [a["attn_q_gain_2"][0], a["attn_k_gain_2"][0], a["attn_sinks_2"][0]])[None, :], (128, NROW)))
    pos = _np.ascontiguousarray(_np.broadcast_to(a["positions"].reshape(1, 256), (128, 256)))
    xT = _np.ascontiguousarray(a["x"][0].T.reshape(8, 128, 256).transpose(1, 0, 2))
    poolw = _np.ascontiguousarray(a["pool_w"][0].transpose(1, 0, 2))

    c = _np.zeros((128, NCONST), _np.float32)
    c[:, C_ID:C_ID + 128] = _np.eye(128)
    i = _np.arange(128)[:, None]
    j = _np.arange(256)[None, :]
    for hd in range(4):
        lg = _np.log1p(-(2.0 ** (-5.0 - hd)))
        c[:, C_DEC + 256 * hd:C_DEC + 256 * hd + 256] = _np.where(
            j >= i, _np.exp(lg * _np.maximum(j - i, 0)), 0.0) * 128.0 ** -0.5
    dist = i + 128 - j
    c[:, C_NEG:C_NEG + 256] = _np.where((dist >= 0) & (dist < 128), -dist, -1e33)
    for g in range(4):
        wnd = 2 << g
        c[:, C_COR + 16 * g:C_COR + 16 * g + 16] = wnd / _np.minimum(_np.arange(16) + 1, wnd)
    f = _np.float32(10000.0) ** (-_np.arange(64, dtype=_np.float32) / _np.float32(64))
    c[:, C_INV] = _np.concatenate([f, f])
    c[0:64, C_SGN] = 1.0
    c[64:128, C_SGN] = -1.0

    nc = _bacc.Bacc("TRN2", target_bir_lowering=False, num_devices=1)
    arrays = {"w": w, "poolw": poolw, "xT": xT, "pos": pos, "cols": cols, "rows": rows, "consts": c}
    aps = [nc.dram_tensor(n, v.shape, _mybir.dt.from_np(v.dtype), kind="ExternalInput").ap()
           for n, v in arrays.items()]
    out = nc.dram_tensor("out", (128, 8, 256), _mybir.dt.float32, kind="ExternalOutput").ap()
    model_kernel(nc, *aps, out)
    r = _run(nc, [arrays], core_ids=[0])
    got = _np.asarray(r.results[0]["out"])
    return _np.ascontiguousarray(got.transpose(1, 0, 2).reshape(1024, 256).T)[None]
```

```python
from contextlib import ExitStack

import numpy as np
import concourse.bass as bass
from concourse import mybir

F32 = mybir.dt.float32
F32R = mybir.dt.float32r
I32 = mybir.dt.int32
ALU = mybir.AluOpType
ACT = mybir.ActivationFunctionType
AX = mybir.AxisListType

P = 128
D = 1024
T = 256
KD = D // P
FF = 2816
KF = FF // P
EPS = 1e-6
PIECE = 1024
CHUNK = 2 * PIECE
RAW = 3
RING = 6
SCR = 12032
TAPS = 12
WIDE = 2
DIAGS = 24

COLS = {}
_at = 0
for _name, _n in (("mix_g", 16), ("ffn_g", 16), ("fin_g", 8), ("ret_g", 4), ("pool_s", 4), ("b_pw1", 16),
                  ("w_dw", 31 * 8), ("b_dw", 8), ("ln_g", 8), ("ln_b", 8), ("b_pw2", 8), ("w_c3", 24),
                  ("mix2_g", 16), ("ffn2_g", 16), ("q_g", 1), ("k_g", 1)):
    COLS[_name] = _at
    _at += _n
NCOL = _at
C_ID, C_DEC, C_NEG, C_COR, C_INV, C_SGN = 0, 128, 128 + 1024, 1536, 1600, 1601
NCONST = 1602
NROW = 16

TWO_PI = 2.0 * np.pi
P1 = 6.28125
P2 = float(np.float32(np.round((TWO_PI - P1) * 2.0**17) / 2.0**17))
P3 = float(np.float32(np.round((TWO_PI - P1 - P2) * 2.0**27) / 2.0**27))
P4 = float(np.float32(TWO_PI - P1 - P2 - P3))
MAGIC = 1.5 * 2.0**23
HALF_PI = float(np.float32(np.pi / 2))
PI_IN = 3.1415925


class Queue:

    def __init__(self, sem):
        self.sem, self.n, self.items, self.seen = sem, 0, [], {}

    def wait(self, *toks):
        for sem, val in toks:
            if self.seen.get(id(sem), 0) < val:
                self.seen[id(sem)] = val
                self.items.append(lambda e, s=sem, v=val: e.wait_ge(s, v))

    def op(self, fn, *toks):
        self.wait(*toks)
        self.n += 1
        self.items.append(lambda e: fn(e).then_inc(self.sem, 1))
        return (self.sem, self.n)

    def raw(self, fn, *toks):
        self.wait(*toks)
        self.items.append(lambda e: fn(e))

    def play(self, e):
        for item in self.items:
            item(e)


class Slots:

    def __init__(self, aps):
        self.aps, self.free, self.i = aps, [[] for _ in aps], -1

    def next(self):
        self.i += 1
        k = self.i % len(self.aps)
        return k, self.aps[k], self.free[k]


def stretch(ap, axis, n):
    shape = list(ap.shape)
    shape.insert(axis, n)
    return ap.unsqueeze(axis).broadcast_to(shape)


def model_kernel(nc, w, poolw, xT, pos, cols, rows, consts, out):
    ctx = ExitStack()
    with ctx:
        def sb(name, shape, dt=F32):
            return ctx.enter_context(nc.sbuf_tensor(name, shape, dt))

        def sem(name):
            return ctx.enter_context(nc.semaphore(name))

        raw_t = sb("raw_t", [P, RAW, CHUNK])
        hi_t = sb("hi_t", [P, RING, PIECE], F32R)
        lo_t = sb("lo_t", [P, RING, PIECE], F32R)
        h = sb("h", [P, KD, T])
        xh = sb("xh", [P, KD, T], F32R)
        xl = sb("xl", [P, KD, T], F32R)
        fh = sb("fh", [P, KF, T], F32R)
        fl = sb("fl", [P, KF, T], F32R)
        cst = sb("cst", [P, NCONST])
        col = sb("col", [P, NCOL])
        row = sb("row", [P, NROW])
        pw = sb("pw", [P, 4, P])
        one = sb("one", [P, P])
        mh = sb("mh", [P, 32])
        rbc = sb("rbc", [P, T])
        rb2 = sb("rb2", [P, T])
        ssum = sb("ssum", [P, T])
        sq = sb("sq", [P, 2, T])
        dg4 = sb("dg", [P, 4, P])
        dg = dg4[:, 0:2, :]
        st = sb("st", [P, 6, 2])
        ssum2 = sb("ssum2", [P, T])
        gg = sb("gg", [P, KD])
        scr = sb("scr", [P, SCR])
        banks = ctx.enter_context(nc.psum_tensor("banks", [P, 8, 512], F32))
        ident = cst[:, C_ID:C_ID + P]

        pe = Queue(sem("s_pe"))
        dve = Queue(sem("s_dve"))
        act = Queue(sem("s_act"))
        pool = Queue(sem("s_pool"))
        sp = Queue(sem("s_sp"))
        s_raw = [sem(f"s_raw{i}") for i in range(RAW)]
        s_ld = {n: sem("s_ld_" + n) for n in ("x0", "x1", "cst", "col", "row", "pw", "pos")}
        s_first = sem("s_first")
        s_out = sem("s_out")

        def colv(name, i):
            return col[:, COLS[name] + i:COLS[name] + i + 1]

        def load(q, name, dst, src):
            q.raw(lambda e: e.dma_start(dst, src).then_inc(s_ld[name], 16))
            return (s_ld[name], 16)

        col_in = load(act, "col", col[:, :], cols)
        x_in = [load(sp, "x0", h[:, 0:4, :], xT[:, 0:4, :])]
        sp.raw(lambda e: e.dma_start(raw_t[:, 0, 0:PIECE], w[0, :, 0:PIECE]).then_inc(s_first, 16))
        x_in.append(load(sp, "x1", h[:, 4:8, :], xT[:, 4:8, :]))
        sp.raw(lambda e: e.dma_start(raw_t[:, 0, PIECE:CHUNK], w[0, :, PIECE:CHUNK]).then_inc(s_raw[0], 16))
        cst_in = load(act, "cst", cst[:, :], consts)
        row_in = load(act, "row", row[:, :], rows)
        posi = scr[:, 0:T].bitcast(I32)
        pos_in = load(act, "pos", posi, pos)
        pw_in = load(act, "pw", pw[:, :, :], poolw)

        n_pieces = w.shape[0] * 2
        hi_tok, lo_tok, freed = {}, {}, {}

        def load_chunk(c):
            if c >= w.shape[0]:
                return
            if c >= RAW:
                for p in (2 * (c - RAW), 2 * (c - RAW) + 1):
                    sp.wait(hi_tok[p], lo_tok[p])
            sp.raw(lambda e: e.dma_start(raw_t[:, c % RAW, :], w[c]).then_inc(s_raw[c % RAW], 16))

        def arrived(p):
            return (s_first, 16) if p == 0 else (s_raw[p // 2 % RAW], 16 * (p // 2 // RAW + 1))

        def slot_free(p):
            return [freed[p - RING]] if p >= RING else []

        def raw_of(p):
            return raw_t[:, p // 2 % RAW, (p % 2) * PIECE:(p % 2 + 1) * PIECE]

        def split_hi(p):
            hi_tok[p] = act.op(lambda e: e.activation(hi_t[:, p % RING, :], raw_of(p), ACT.Copy), arrived(p),
                               *slot_free(p))

        def split_lo(p):
            lo_tok[p] = dve.op(lambda e: e.tensor_tensor(lo_t[:, p % RING, :], raw_of(p),
                                                         hi_t[:, p % RING, :].bitcast(F32), ALU.subtract),
                               arrived(p), *slot_free(p), hi_tok[p])
            if p % 2:
                load_chunk(p // 2 + RAW)

        class Stream:
            g = 0
            flushed = 0

            @classmethod
            def take(cls, n):
                p, r = cls.g // 8, cls.g % 8
                cls.g += n
                if r >= 3 and cls.flushed < p:
                    cls.flushed = p
                    flush()
                s = slice(r * P, (r + n) * P)
                return p, hi_t[:, p % RING, s], lo_t[:, p % RING, s], (r + n == 8)

        pending, lo_next, later = [], [], []

        def release(p, tok):
            freed[p] = tok
            if p - 1 + RING < n_pieces:
                pending.append(p - 1 + RING)

        def flush():
            while pending:
                split_hi(pending[0])
                if lo_next:
                    split_lo(lo_next.pop(0))
                lo_next.append(pending.pop(0))
            if len(freed) >= n_pieces - RING:
                while lo_next:
                    split_lo(lo_next.pop(0))
            if later:
                later.pop(0)()

        def drain():
            while later:
                later.pop(0)()

        bank_free = [[] for _ in range(8)]
        idle = list(range(8))

        def bank():
            b = idle.pop(0)
            pe.wait(*bank_free[b])
            return b, banks[:, b, :]

        def free_bank(b, *toks):
            bank_free[b] = list(toks)
            idle.append(b)

        def mm(out_, l, r_, start, stop, inc=False, toks=(), skip=False):
            fn = lambda e: e.matmul(out_, l, r_, start=start, stop=stop, skip_group_check=skip)
            if inc:
                return pe.op(fn, *toks)
            pe.raw(fn, *toks)

        def mm3(out_, wt, a_hi, a_lo, toks, first, last, stationary_w, end=None, skip=False):
            p, w_hi, w_lo, ends = wt
            end = ends if end is None else end
            pairs = ((w_hi, a_hi), (w_hi, a_lo), (w_lo, a_hi))
            tok = None
            for i, (a, b) in enumerate(pairs):
                need = (hi_tok[p], toks[0]) if i == 0 else ((toks[1],) if i == 1 else (lo_tok[p],))
                l, r_ = (a, b) if stationary_w else (b, a)
                tok = mm(out_, l, r_, first and i == 0, last and i == 2, inc=(i == 2 and (end or last)), toks=need, skip=skip)
            if end:
                release(p, tok)
            return tok

        def product(nk, units, a_hi, a_lo, a_tok, evac, hooks=None, wide=1):
            hooks = dict(hooks or {})
            late, count = [], 0
            ready = not hooks
            for u in [0] + list(range(wide, len(units))):
                group = list(range(u, u + (wide if u == 0 else 1)))
                open_banks = [bank() for _ in group]
                one_k = [(ps, t) for (b, ps), v in zip(open_banks, group) for t in range(units[v])]
                if u == 0 and wide > 1:
                    order = [(k, ps, t) for k in range(nk) for ps, t in one_k]
                else:
                    order = [(k, ps, t) for ps, t in one_k for k in range(nk)]
                toks = {}
                for k, ps, t in order:
                    if a_tok[k] is None or a_tok[k][1] is None:
                        drain()
                    wt = Stream.take(1)
                    tok = mm3(ps[:, t * T:(t + 1) * T], wt, a_hi[:, k, :], a_lo[:, k, :], a_tok[k],
                              k == 0 and (wide == 1 or u > 0 or t == 0), k == nk - 1, True, skip=wide > 1)
                    count += 1
                    if count in hooks:
                        ready = hooks.pop(count)() or ready
                        if ready:
                            for item in late:
                                evac(*item)
                            late = []
                    if k == nk - 1:
                        toks[id(ps)] = tok
                for v, (b, ps) in zip(group, open_banks):
                    late.append((v, b, ps, toks[id(ps)]))
                if ready:
                    for item in late:
                        evac(*item)
                    late = []
            assert not late and not hooks

        ones_tok = dve.op(lambda e: e.memset(one[:, :], 1.0))
        mh_tok = pool.op(lambda e: e.memset(mh[:, :], -0.5))
        x_tok = [None] * KD
        ss = {}

        sqs = Slots([sq[:, 0, :], sq[:, 1, :]])

        def prep(k, gain, src_tok, put_off, squares=None):
            x_tok[k] = None
            a = act.op(lambda e: e.activation(xh[:, k, :], h[:, k, :], ACT.Copy, scale=gain(k)), *src_tok, col_in)

            def lo():
                b = dve.op(lambda e: e.scalar_tensor_tensor(xl[:, k, :], h[:, k, :], gain(k),
                                                            xh[:, k, :].bitcast(F32), ALU.mult, ALU.subtract), a)
                x_tok[k] = (a, b)

            def square():
                one_square(k, ssum, "t", src_tok, None)
                if squares:
                    one_square(k, ssum2, "t2", src_tok, squares)

            if put_off:
                later.append(lo)
            else:
                lo()
            later.append(square)

        def one_square(k, dst, key, src_tok, scale):
            by = {} if scale is None else {"scale": scale(k)}
            if k == 0:
                ss[key] = act.op(lambda e: e.activation(dst[:, :], h[:, 0, :], ACT.Square, **by), *src_tok,
                                 *ss.get("read", []))
            else:
                i, buf, free = sqs.next()
                s = act.op(lambda e: e.activation(buf, h[:, k, :], ACT.Square, **by), *src_tok, *free)
                ss[key] = dve.op(lambda e: e.tensor_tensor(dst[:, :], dst[:, :], buf, ALU.add), s, ss[key])
                sqs.free[i] = [ss[key]]

        def gain_of(name, first):
            return lambda k: colv(name, first + k)

        rs = {"used": [], "st": []}

        def rms_a(diagonals=True):
            drain()
            b, ps = bank()
            for i in range(2):
                tok = mm(ps[:, i:i + 1], ssum[:, i * P:(i + 1) * P], one[:, 0:1], True, True, inc=True,
                         toks=(ss["t"], ones_tok))
            ss["read"] = [tok]
            a = dve.op(lambda e: e.tensor_scalar(st[:, 0, :], ps[:, 0:2], 1.0 / D, EPS, ALU.mult, ALU.add), tok)
            free_bank(b, a)
            c = pool.op(lambda e: e.tensor_tensor(st[:, 1, :], st[:, 0, :], mh[:, 0:2], ALU.pow), a, mh_tok,
                        *rs["st"])
            rs["st"] = []
            rs["pow"] = c
            for i in range(2 if diagonals else 0):
                rs["dg"] = dve.op(lambda e, i=i: e.tensor_scalar(dg[:, i, :], ident, st[:, 1, i:i + 1], None, ALU.mult),
                                  c, cst_in)

        def rms_b(square=False):
            b, ps = bank()
            tok = mm(ps[:, 0:T], one[:, :], dg[:, :, :].rearrange("p a b -> p (a b)"), True, True, inc=True,
                     toks=(rs["dg"],))
            rs["t"] = dve.op(lambda e: e.tensor_copy(rbc[:, :], ps[:, 0:T]), tok, *rs["used"])
            free_bank(b, rs["t"])
            rs["used"] = []
            if square:
                rs["t"] = dve.op(lambda e: e.tensor_tensor(rb2[:, :], rbc[:, :], rbc[:, :], ALU.mult), rs["t"])

        def double_a():
            drain()
            b, ps = bank()
            for n, sums in enumerate((ssum, ssum2)):
                for i in range(2):
                    tok = mm(ps[:, 2 * n + i:2 * n + i + 1], sums[:, i * P:(i + 1) * P], one[:, 0:1], True, True,
                             inc=True, toks=(ss["t"], ss["t2"]))
            ss["read"] = [tok]
            rs["h_read"] = [ss["t"], ss["t2"], x_tok[KD - 1][1]]
            a = dve.op(lambda e: e.tensor_scalar(st[:, 0, :], ps[:, 0:2], 1.0 / D, EPS, ALU.mult, ALU.add), tok,
                       rs["pow"])
            m2 = dve.op(lambda e: e.tensor_scalar(st[:, 2, :], ps[:, 2:4], 1.0 / D, None, ALU.mult))
            free_bank(b, m2)
            r1 = pool.op(lambda e: e.tensor_tensor(st[:, 3, :], st[:, 0, :], mh[:, 0:2], ALU.pow), a)
            t = pool.op(lambda e: e.tensor_tensor(st[:, 4, :], st[:, 3, :], st[:, 3, :], ALU.mult), r1)
            t = pool.op(lambda e: e.tensor_tensor(st[:, 4, :], st[:, 4, :], st[:, 2, :], ALU.mult), t, m2)
            t = pool.op(lambda e: e.tensor_scalar(st[:, 4, :], st[:, 4, :], EPS, None, ALU.add), t)
            t = pool.op(lambda e: e.tensor_tensor(st[:, 5, :], st[:, 4, :], mh[:, 0:2], ALU.pow), t)
            t = pool.op(lambda e: e.tensor_tensor(st[:, 1, :], st[:, 3, :], st[:, 5, :], ALU.mult), t)
            for n in range(4):
                src = st[:, 3 if n < 2 else 1, n % 2:n % 2 + 1]
                rs["dg"] = dve.op(lambda e, n=n, src=src: e.tensor_scalar(dg4[:, n, :], ident, src, None, ALU.mult),
                                  t, cst_in, *rs.get("dg_free", []))

        def rms_hooks(a=24, b=36, extra=None):
            def last():
                rms_b()
                if extra:
                    extra()
                return True
            return {a: rms_a, b: last}

        def scratch(off, n):
            return scr[:, off:off + n]

        f_tok = [None] * KF

        def put_hi(k, src, tok):
            f_tok[k] = (act.op(lambda e: e.activation(fh[:, k, :], src, ACT.Copy), tok), None)

        def put_lo(k, src):
            a = f_tok[k][0]
            f_tok[k] = (a, dve.op(lambda e: e.tensor_tensor(fl[:, k, :], src, fh[:, k, :].bitcast(F32),
                                                            ALU.subtract), a))
            return f_tok[k][1]

        def put_f(k, src, toks, n=1):
            a = act.op(lambda e: e.activation(fh[:, k:k + n, :], src, ACT.Copy), *toks)
            b = dve.op(lambda e: e.tensor_tensor(fl[:, k:k + n, :], src, fh[:, k:k + n, :].bitcast(F32),
                                                 ALU.subtract), a)
            for i in range(n):
                f_tok[k + i] = (a, b)
            return b

        def ffn(next_gain, squares=None):
            t_ring = Slots([scratch(i * 512, 512) for i in range(3)])
            s_ring = Slots([scratch(1536 + i * T, T) for i in range(2)])
            m_ring = Slots([scratch(2048 + i * T, T) for i in range(2)])
            begun, ended = [], [0]

            def up(u, b, ps, tok):
                f_tok[u] = None
                while len(begun) > ended[0] + 1:
                    later.pop(0)()
                begun.append(u)
                i, t, free = t_ring.next()
                j, s, sfree = s_ring.next()
                l, m, mfree = m_ring.next()
                tv = t.rearrange("p (a b) -> p a b", a=2)
                a = dve.op(lambda e: e.tensor_tensor(tv, ps.rearrange("p (a b) -> p a b", a=2),
                                                     stretch(rbc[:, :], 1, 2), ALU.mult), tok, rs["t"], *free)
                free_bank(b, a)
                rs["used"] = [a]
                c = act.op(lambda e: e.activation(s, t[:, 0:T], ACT.Silu), a, *sfree)

                def gate():
                    d = dve.op(lambda e: e.tensor_tensor(m, s, t[:, T:2 * T], ALU.mult), c, *mfree)
                    t_ring.free[i] = s_ring.free[j] = [d]
                    put_hi(u, m, d)

                def rest():
                    m_ring.free[l] = [put_lo(u, m)]
                    ended[0] += 1

                later.extend((gate, rest))

            product(KD, [2] * KF, xh, xl, x_tok, up, rms_hooks(), wide=WIDE)

            def down(u, b, ps, tok):
                a = dve.op(lambda e: e.tensor_tensor(h[:, u, :], ps[:, 0:T], h[:, u, :], ALU.add), tok)
                free_bank(b, a)
                if next_gain:
                    prep(u, next_gain, (a,), u < 7, squares)
                else:
                    sp.raw(lambda e: e.dma_start(out[:, u, :], h[:, u, :]).then_inc(s_out, 16), a)

            product(KF, [1] * KD, fh, fl, f_tok, down)

        class OutProduct:

            def __init__(self, order, n_outer, next_gain, bias=None):
                self.order, self.n_outer = order, n_outer
                self.next_gain, self.bias = next_gain, bias
                self.banks, self.done, self.at = None, 0, 0

            def block(self, j, n):
                if self.banks is None:
                    self.banks = [bank() for _ in range(4)]
                    drain()
                k = self.order[n]
                wt = Stream.take(1)
                ps = self.banks[j // 2][1][:, (j % 2) * T:(j % 2 + 1) * T]
                return mm3(ps, wt, fh[:, k, :], fl[:, k, :], f_tok[k], n == 0 and j % 2 == 0, n == KD - 1, True,
                           skip=True)

            def outer(self, blocks=8):
                for _ in range(blocks):
                    self.block(self.at, self.done)
                    self.at += 1
                    if self.at == 8:
                        self.at, self.done = 0, self.done + 1

            def finish(self):
                while self.done < self.n_outer:
                    self.outer(8 - self.at)
                for pair in range(4):
                    for j in (2 * pair, 2 * pair + 1):
                        for n in range(self.n_outer, KD):
                            tok = self.block(j, n)
                    b, ps = self.banks[pair]
                    bias = self.bias
                    pair_h = h[:, 2 * pair:2 * pair + 2, :]
                    if bias is None:
                        a = dve.op(lambda e, pair_h=pair_h, ps=ps: e.tensor_tensor(pair_h, ps.rearrange("p (a b) -> p a b", a=2), pair_h,
                                                             ALU.add), tok)
                    else:
                        for j in (2 * pair, 2 * pair + 1):
                            src = ps[:, (j % 2) * T:(j % 2 + 1) * T]
                            a = dve.op(lambda e, bias=bias, j=j, src=src: e.scalar_tensor_tensor(
                                h[:, j, :], src, colv(bias, j), h[:, j, :], ALU.add, ALU.add), tok, col_in)
                    free_bank(b, a)
                    for j in (2 * pair, 2 * pair + 1):
                        prep(j, self.next_gain, (a,), pair < 3)

        def retention():
            cos, sin = scratch(0, T), scratch(T, T)
            w0, w1 = scratch(2 * T, T), scratch(3 * T, T)
            cosr, sinr = scratch(4 * T, T), scratch(5 * T, T)
            qk = scratch(6 * T, 8 * T).rearrange("p (a b) -> p a b", a=8)
            vt = scratch(14 * T, 4 * T).rearrange("p (a b) -> p a b", a=2)
            gs = scratch(18 * T, 4 * T).rearrange("p (a b) -> p a b", a=4)
            UP = 16 + T
            up = scratch(22 * T, 4 * UP).rearrange("p (a b) -> p a b", a=4)
            o0 = 22 * T + 4 * UP
            ta = Slots([scratch(o0 + i * 512, 512) for i in range(2)])
            tb = Slots([scratch(o0 + 1024 + i * 512, 512) for i in range(2)])
            o1 = o0 + 2048
            sT = scratch(o1, 4 * 384).rearrange("p (a b) -> p a b", a=4)
            o2 = o1 + 4 * 384
            assert o2 <= SCR
            posf = w0
            t = dve.op(lambda e: e.tensor_copy(posf, posi), pos_in)
            ang = w1
            t = dve.op(lambda e: e.tensor_scalar(ang, posf, cst[:, C_INV:C_INV + 1], None, ALU.mult), t, cst_in)
            kk = cosr
            t = dve.op(lambda e: e.tensor_scalar(kk, ang, float(1 / TWO_PI), MAGIC, ALU.mult, ALU.add), t)
            t = dve.op(lambda e: e.tensor_scalar(kk, kk, MAGIC, None, ALU.subtract), t)
            for c in (P1, P2, P3, P4):
                t = dve.op(lambda e, c=c: e.scalar_tensor_tensor(ang, kk, -c, ang, ALU.mult, ALU.add), t)
            t = dve.op(lambda e: e.tensor_scalar(kk, ang, HALF_PI, float(-TWO_PI), ALU.is_gt, ALU.mult), t)
            t2 = dve.op(lambda e: e.scalar_tensor_tensor(w0, ang, HALF_PI, kk, ALU.add, ALU.add), t)
            t = dve.op(lambda e: e.tensor_scalar(w1, ang, PI_IN, -PI_IN, ALU.min, ALU.max), t2)
            t2 = dve.op(lambda e: e.tensor_scalar(w0, w0, PI_IN, -PI_IN, ALU.min, ALU.max), t2)
            sin_t = act.op(lambda e: e.activation(sin, w1, ACT.Sin, scale=cst[:, C_SGN:C_SGN + 1]), t, t2)
            cos_t = act.op(lambda e: e.activation(cos, w0, ACT.Sin), t2)
            pad_t = pool.op(lambda e: e.memset(up[:, :, 0:16], 0.0))
            rr = {}

            def tables():
                a = dve.op(lambda e: e.tensor_tensor(cosr, cos, rbc[:, :], ALU.mult), cos_t, rs["t"])
                rr["t"] = dve.op(lambda e: e.tensor_tensor(sinr, sin, rbc[:, :], ALU.mult), sin_t, a)

            qk_tok = {}

            def two(ap):
                return ap.rearrange("p (a b) -> p a b", a=2)

            def qk_evac(u, b, ps, tok):
                i, a_, afree = ta.next()
                j, b_, bfree = tb.next()
                a = dve.op(lambda e: e.tensor_tensor(two(a_), two(ps), stretch(cosr, 1, 2), ALU.mult),
                           tok, rr["t"], *afree)
                c = dve.op(lambda e: e.tensor_tensor(two(b_)[0:64], two(ps)[64:128],
                                                     stretch(sinr[64:128], 1, 2), ALU.mult), *bfree)
                c2 = dve.op(lambda e: e.tensor_tensor(two(b_)[64:128], two(ps)[0:64],
                                                      stretch(sinr[0:64], 1, 2), ALU.mult))
                free_bank(b, c2)
                d = dve.op(lambda e: e.tensor_tensor(qk[:, 2 * u:2 * u + 2, :], two(a_), two(b_), ALU.add), a, c2)
                ta.free[i] = tb.free[j] = [d]
                qk_tok[u] = d

            product(KD, [2] * 4, xh, xl, x_tok, qk_evac, rms_hooks(extra=tables))

            vb = [bank(), bank()]
            for k in range(KD):
                wt = Stream.take(4)
                for i in range(2):
                    vtok = mm3(vb[i][1], wt, xh[:, k, i * P:(i + 1) * P], xl[:, k, i * P:(i + 1) * P], x_tok[k],
                               k == 0, k == KD - 1, False, end=(i == 1 and wt[3]))
            v_tok = []
            for i in range(2):
                a = dve.op(lambda e, i=i: e.tensor_scalar(vt[:, i, :], vb[i][1], st[:, 1, i:i + 1], None, ALU.mult),
                           vtok, rs["pow"])
                free_bank(vb[i][0], a)
                v_tok.append(a)
            rs["st"] = [v_tok[1]]

            u_tok = {}

            def u_evac(u, b, ps, tok):
                a = dve.op(lambda e: e.tensor_tensor(up[:, 2 * u:2 * u + 2, 16:UP], two(ps),
                                                     stretch(rbc[:, :], 1, 2), ALU.mult), tok, rs["t"])
                free_bank(b, a)
                u_tok[u] = a

            product(KD, [2, 2], xh, xl, x_tok, u_evac)
            y_tok = []
            y_ap = [cos, sin, cosr, sinr]
            wide = Slots([scratch(o1, UP), scratch(o1 + UP, UP)])
            for gi in range(4):
                cur, t = up[:, gi, :], u_tok[gi // 2]
                n = gi + 1
                for s in range(n):
                    sh = 1 << s
                    i, dst, free = wide.next()
                    lo = 2 * sh - 1
                    t2 = pool.op(lambda e, dst=dst, cur=cur, sh=sh, lo=lo: e.tensor_tensor(
                        dst[:, lo:UP], cur[:, lo:UP], cur[:, lo - sh:UP - sh], ALU.add),
                        t, pad_t, *free)
                    cur, t = dst, t2
                    wide.free[i] = []
                t = pool.op(lambda e, cur=cur, gi=gi: e.tensor_tensor(
                    cur[:, 16:32], cur[:, 16:32], cst[:, C_COR + 16 * gi:C_COR + 16 * gi + 16], ALU.mult), t, cst_in)
                t = dve.op(lambda e, cur=cur, gi=gi: e.scalar_tensor_tensor(
                    y_ap[gi], cur[:, 16:UP], 1.0 / (2 << gi), up[:, gi, 16:UP], ALU.mult, ALU.subtract),
                    t, *qk_tok.values())
                wide.free[wide.i % 2] = [t]
                y_tok.append(t)
            wide_done = y_tok[3]

            s_tok = []
            for hd in range(4):
                b, ps = bank()
                mm(ps[:, 0:T], qk[:, 4 + hd, 0:P], qk[:, hd, :], True, True,
                   toks=(qk_tok[hd // 2], qk_tok[2 + hd // 2]))
                tok = mm(ps[:, T:T + P], qk[:, 4 + hd, P:T], qk[:, hd, P:T], True, True, inc=True)
                dec = cst[:, C_DEC + T * hd:C_DEC + T * hd + T]
                a = dve.op(lambda e, hd=hd, ps=ps, dec=dec: e.tensor_tensor(sT[:, hd, 0:T], ps[:, 0:T], dec, ALU.mult),
                           tok, wide_done)
                a = dve.op(lambda e, hd=hd, ps=ps, dec=dec: e.tensor_tensor(sT[:, hd, T:T + P], ps[:, T:T + P],
                                                                            dec[:, 0:P], ALU.mult))
                free_bank(b, a)
                s_tok.append(a)
            gs_tok = {}

            def g_evac(u, b, ps, tok):
                i, a_, afree = ta.next()
                a = dve.op(lambda e: e.tensor_tensor(two(a_), two(ps), stretch(rbc[:, :], 1, 2), ALU.mult),
                           tok, rs["t"], *afree)
                free_bank(b, a)
                rs["used"] = [a]
                c = act.op(lambda e: e.activation(gs[:, 2 * u:2 * u + 2, :], two(a_), ACT.Silu), a)
                ta.free[i] = [c]
                gs_tok[u] = c

            product(KD, [2, 2], xh, xl, x_tok, g_evac)

            oT = qk[:, 0:4, :]
            o2 = qk[:, 4:8, :]
            o_tok = []
            for pr in range(2):
                b, ps = bank()
                for i in range(2):
                    hd = 2 * pr + i
                    vs = [vt[:, m, hd * P:(hd + 1) * P] for m in range(2)]
                    mm(ps[:, i * T:(i + 1) * T], vs[0], sT[:, hd, 0:T], True, False, toks=(s_tok[hd], v_tok[1]))
                    tok = mm(ps[:, i * T + P:(i + 1) * T], vs[1], sT[:, hd, T:T + P], False, True, inc=True)
                a = dve.op(lambda e, pr=pr, ps=ps: e.tensor_copy(oT[:, 2 * pr:2 * pr + 2, :], two(ps)), tok)
                free_bank(b, a)
                o_tok.append(a)
            for half in range(2):
                b, ps = bank()
                for i in range(2):
                    gi = 2 * half + i
                    tok = mm(ps[:, i * T:(i + 1) * T], pw[:, gi, :], y_ap[gi], True, True, inc=True,
                             toks=(pw_in, y_tok[gi]))
                for i in range(2):
                    gi = 2 * half + i
                    a = act.op(lambda e, gi=gi, i=i, ps=ps: e.activation(
                        fh[:, 4 + gi, :], ps[:, i * T:(i + 1) * T], ACT.Copy, scale=colv("pool_s", gi)), tok, col_in)
                for i in range(2):
                    gi = 2 * half + i
                    c = dve.op(lambda e, gi=gi, i=i, ps=ps: e.scalar_tensor_tensor(
                        fl[:, 4 + gi, :], ps[:, i * T:(i + 1) * T], colv("pool_s", gi),
                        fh[:, 4 + gi, :].bitcast(F32), ALU.mult, ALU.subtract), a)
                    f_tok[4 + gi] = (a, c)
                free_bank(b, a, c)
            product_out = OutProduct((4, 5, 6, 7, 0, 1, 2, 3), 4, gain_of("ffn_g", 0))
            product_out.outer(4)
            sq_tok, d_tok = [], []
            for pr in range(2):
                b, ps = bank()
                tok = mm(ps, one[:, :], oT[:, 2 * pr:2 * pr + 2, :], True, True, inc=True, toks=(o_tok[pr],))
                a = dve.op(lambda e, pr=pr, ps=ps: e.scalar_tensor_tensor(
                    oT[:, 2 * pr:2 * pr + 2, :], two(ps), -1.0 / P, oT[:, 2 * pr:2 * pr + 2, :], ALU.mult, ALU.add),
                    tok)
                free_bank(b, a)
                d_tok.append(a)
                sq_tok.append(act.op(lambda e, pr=pr, o2=o2: e.activation(o2[:, 2 * pr:2 * pr + 2, :],
                                                                   oT[:, 2 * pr:2 * pr + 2, :], ACT.Square), a))
                product_out.outer(8)
            b, ps = bank()
            for hd in range(4):
                for i in range(2):
                    tok = mm(ps[:, 2 * hd + i:2 * hd + i + 1], o2[:, hd, i * P:(i + 1) * P], one[:, 0:1], True, True,
                             inc=True, toks=(sq_tok[hd // 2],))
            gst = up[:, 0, 0:16]
            a = dve.op(lambda e, ps=ps: e.tensor_scalar(gst[:, 0:8], ps[:, 0:8], 1.0 / P, EPS, ALU.mult, ALU.add), tok,
                       *y_tok)
            free_bank(b, a)
            c = pool.op(lambda e: e.tensor_tensor(gst[:, 8:16], gst[:, 0:8], mh[:, 0:8], ALU.pow), a)
            dgs = sT.rearrange("p a b -> p (a b)")
            product_out.outer(12)
            for i in range(8):
                dtok = dve.op(lambda e, i=i: e.tensor_scalar(dgs[:, i * P:(i + 1) * P], ident, gst[:, 8 + i:9 + i],
                                                             None, ALU.mult), c, tok)
            for pr in range(2):
                b, ps = bank()
                tok = mm(ps, one[:, :], dgs[:, pr * 512:(pr + 1) * 512], True, True, inc=True, toks=(dtok,))
                a = dve.op(lambda e, pr=pr, ps=ps: e.tensor_tensor(
                    oT[:, 2 * pr:2 * pr + 2, :], two(ps), oT[:, 2 * pr:2 * pr + 2, :], ALU.mult), tok,
                    sq_tok[pr])
                free_bank(b, a)
                for i in range(2):
                    hd = 2 * pr + i
                    c = dve.op(lambda e, hd=hd: e.scalar_tensor_tensor(
                        oT[:, hd, :], oT[:, hd, :], colv("ret_g", hd), gs[:, hd, :], ALU.mult, ALU.mult),
                        a, gs_tok[pr])
                    put_f(hd, oT[:, hd, :], (c,))
            product_out.finish()

        def conformer():
            UP = 32 + T
            u_r = Slots([scratch(i * UP, UP) for i in range(3)])
            o0 = 3 * UP
            t_ring = Slots([scratch(o0 + i * 512, 512) for i in range(2)])
            s_ring = Slots([scratch(o0 + 1024 + i * T, T) for i in range(2)])
            o1 = o0 + 1024 + 2 * T
            dw = scratch(o1, 8 * T).rearrange("p (a b) -> p a b", a=8)
            o2 = o1 + 8 * T
            acc2 = [scratch(o2 + i * T, T) for i in range(2)]
            o3 = o2 + 2 * T
            dsq = scratch(o3, 8 * T).rearrange("p (a b) -> p a b", a=8)
            o4 = o3 + 8 * T
            dgr = Slots([scratch(o4 + i * P, P) for i in range(DIAGS)])
            assert o4 + DIAGS * P <= SCR
            pads = [pool.op(lambda e, i=i: e.memset(u_r.aps[i][:, 0:32], 0.0), f_tok[KF - 1][1]) for i in range(3)]
            dw_tok = [None] * 8

            def evac(u, b, ps, tok):
                i, t, free = t_ring.next()
                j, s, sfree = s_ring.next()
                l, ub, ufree = u_r.next()
                u_r.free[l] = []
                a = dve.op(lambda e: e.tensor_tensor(t.rearrange("p (a b) -> p a b", a=2),
                                                     ps.rearrange("p (a b) -> p a b", a=2),
                                                     stretch(rbc[:, :], 1, 2), ALU.mult), tok, rs["t"], *free)
                free_bank(b, a)
                rs["used"] = [a]
                c = act.op(lambda e: e.activation(s, t[:, T:2 * T], ACT.Sigmoid, bias=colv("b_pw1", 8 + u)), a,
                           *sfree)
                d = dve.op(lambda e: e.scalar_tensor_tensor(ub[:, 32:UP], t[:, 0:T], colv("b_pw1", u), s,
                                                            ALU.add, ALU.mult), c, pads[l], *ufree)
                t_ring.free[i] = s_ring.free[j] = [d]
                diags = []
                for k in range(TAPS):
                    i, dgk, dfree = dgr.next()
                    x = act.op(lambda e, dgk=dgk, k=k: e.activation(dgk, ident, ACT.Copy, scale=colv("w_dw", 8 * k + u)),
                               cst_in, col_in, f_tok[KF - 1][1], *dfree)
                    diags.append((i, dgk, k, x))
                todo.append((u, l, ub, d, diags))
                if u >= 1:
                    taps()
                acc = [dw[:, u, :], acc2[u % 2]]
                ct = [None, None]
                for n, k in enumerate(range(TAPS, 31)):
                    q = n % 2
                    if n == 8 and u >= 1:
                        add_taps(u - 1)
                    src = ub[:, 2 + k:2 + k + T]
                    wk = colv("w_dw", 8 * k + u)
                    if n == 0:
                        ct[0] = dve.op(lambda e, src=src, wk=wk: e.tensor_scalar(acc[0], src, wk, colv("b_dw", u), ALU.mult, ALU.add),
                                       d)
                    elif n == 1:
                        ct[1] = dve.op(lambda e, src=src, wk=wk: e.tensor_scalar(acc[1], src, wk, None, ALU.mult), d)
                    else:
                        ct[q] = dve.op(lambda e, q=q, src=src, wk=wk: e.scalar_tensor_tensor(acc[q], src, wk, acc[q], ALU.mult, ALU.add),
                                       ct[q])
                u_r.free[l] += [ct[0], ct[1]]
                sums[u] = dve.op(lambda e: e.tensor_tensor(acc[0], acc[0], acc[1], ALU.add), ct[0], ct[1])
                if u >= 2:
                    mean(u - 2)

            todo, sums, tap_bank = [], {}, {}
            mean_bank = []

            def taps():
                u, l, ub, d, diags = todo.pop(0)
                b, ps = bank()
                for n, (i, dgk, k, x) in enumerate(diags):
                    tok = mm(ps[:, 0:T], dgk, ub[:, 2 + k:2 + k + T], n == 0, n == TAPS - 1, inc=True, toks=(x, d))
                    dgr.free[i] = [tok]
                u_r.free[l].append(tok)
                tap_bank[u] = b, ps, tok

            def add_taps(u):
                b, ps, tok = tap_bank.pop(u)
                dw_tok[u] = dve.op(lambda e: e.tensor_tensor(dw[:, u, :], ps[:, 0:T], dw[:, u, :], ALU.add), tok,
                                   sums[u])
                free_bank(b, dw_tok[u])

            def mean(u):
                if not mean_bank:
                    mean_bank.append(bank())
                return mm(mean_bank[0][1][:, 0:T], one[:, :], dw[:, u, :], u == 0, u == 7, inc=True,
                          toks=(dw_tok[u],))

            product(KD, [2] * KD, xh, xl, x_tok, evac, rms_hooks(10, 20))
            taps()
            mean(6)
            add_taps(7)
            tok = mean(7)
            b, ps = mean_bank[0]
            q_tok = []
            for i in range(4):
                a = dve.op(lambda e, i=i, ps=ps: e.scalar_tensor_tensor(
                    dw[:, 2 * i:2 * i + 2, :], stretch(ps[:, 0:T], 1, 2), -1.0 / D, dw[:, 2 * i:2 * i + 2, :],
                    ALU.mult, ALU.add), tok)
                q_tok.append(act.op(lambda e, i=i: e.activation(dsq[:, 2 * i:2 * i + 2, :], dw[:, 2 * i:2 * i + 2, :],
                                                                ACT.Square), a))
            free_bank(b, a)
            a = dve.op(lambda e: e.tensor_tensor(dsq[:, 0:2, :], dsq[:, 0:2, :], dsq[:, 2:4, :], ALU.add), q_tok[0], q_tok[1])
            a = dve.op(lambda e: e.tensor_tensor(dsq[:, 0:2, :], dsq[:, 0:2, :], dsq[:, 4:6, :], ALU.add), a, q_tok[2])
            a = dve.op(lambda e: e.tensor_tensor(dsq[:, 0:2, :], dsq[:, 0:2, :], dsq[:, 6:8, :], ALU.add), a, q_tok[3])
            a = dve.op(lambda e: e.tensor_tensor(dsq[:, 0, :], dsq[:, 0, :], dsq[:, 1, :], ALU.add), a)
            b, ps = bank()
            for i in range(2):
                tok = mm(ps[:, i:i + 1], dsq[:, 0, i * P:(i + 1) * P], one[:, 0:1], True, True, inc=True, toks=(a,))
            sq_read = tok
            a = dve.op(lambda e, ps=ps: e.tensor_scalar(st[:, 0, :], ps[:, 0:2], 1.0 / D, EPS, ALU.mult, ALU.add), tok)
            free_bank(b, a)
            c = pool.op(lambda e: e.tensor_tensor(st[:, 1, :], st[:, 0, :], mh[:, 0:2], ALU.pow), a)
            for i in range(2):
                d = dve.op(lambda e, i=i: e.tensor_scalar(dg[:, i, :], ident, st[:, 1, i:i + 1], None, ALU.mult), c)
            b, ps = bank()
            tok = mm(ps[:, 0:T], one[:, :], dg[:, :, :].rearrange("p a b -> p (a b)"), True, True, inc=True,
                     toks=(d,))
            product_out = OutProduct(range(KD), 3, gain_of("ffn_g", 8), bias="b_pw2")
            for i in range(4):
                a = dve.op(lambda e, i=i, ps=ps: e.tensor_tensor(
                    dw[:, 2 * i:2 * i + 2, :], stretch(ps[:, 0:T], 1, 2), dw[:, 2 * i:2 * i + 2, :], ALU.mult), tok,
                    q_tok[i])
                for j in (2 * i, 2 * i + 1):
                    s = act.op(lambda e, j=j: e.activation(dsq[:, j, :], dw[:, j, :], ACT.Silu,
                                                           scale=colv("ln_g", j), bias=colv("ln_b", j)), a, sq_read)
                    put_f(j, dsq[:, j, :], (s,))
                if i == 3:
                    free_bank(b, a)
                if i < 2:
                    product_out.outer(8 + 4 * i)
            product_out.finish()

        def short_conv():
            UP = 8 + T
            u_r = Slots([scratch(i * UP, UP) for i in range(2)])
            o0 = 2 * UP
            tb = Slots([scratch(o0 + i * T, T) for i in range(2)])
            tc = Slots([scratch(o0 + 2 * T + i * T, T) for i in range(2)])
            y_r = Slots([scratch(o0 + 4 * T + i * T, T) for i in range(2)])
            pads = [pool.op(lambda e, i=i: e.memset(u_r.aps[i][:, 0:8], 0.0), f_tok[KF - 1][1]) for i in range(2)]
            y_of = {}

            def evac(u, b, ps, tok):
                j = u // 2
                if u % 2 == 0:
                    i, t, free = tb.next()
                    l, ub, ufree = u_r.next()
                    m, y, yfree = y_r.next()
                    a = dve.op(lambda e, t=t: e.tensor_tensor(t, ps[:, 0:T], rb2[:, :], ALU.mult), tok, rs["t"], *free)
                    c = dve.op(lambda e, t=t: e.tensor_tensor(ub[:, 8:UP], ps[:, T:2 * T], t, ALU.mult), a, pads[l],
                               *ufree)
                    free_bank(b, c)
                    tb.free[i] = [c]
                    d = act.op(lambda e, y=y: e.activation(y, ub[:, 6:6 + T], ACT.Copy, scale=colv("w_c3", j)), c,
                               *yfree)

                    def taps():
                        f = dve.op(lambda e: e.scalar_tensor_tensor(y, ub[:, 7:7 + T], colv("w_c3", 8 + j), y,
                                                                    ALU.mult, ALU.add), d)
                        f = dve.op(lambda e: e.scalar_tensor_tensor(y, ub[:, 8:8 + T], colv("w_c3", 16 + j), y,
                                                                    ALU.mult, ALU.add), f)
                        u_r.free[l] = [f]
                        y_of[j] = (m, y, f)

                    later.append(taps)
                else:
                    if j not in y_of:
                        drain()
                    m, y, yt = y_of[j]
                    i, t, free = tc.next()
                    a = dve.op(lambda e, t=t: e.tensor_tensor(t, ps[:, 0:T], rbc[:, :], ALU.mult), tok, rs["t"], *free)
                    free_bank(b, a)
                    rs["used"] = [a]


                    def gate():
                        c = dve.op(lambda e: e.tensor_tensor(t, t, y, ALU.mult), a, yt)
                        y_r.free[m] = [c]
                        put_hi(j, t, c)

                    def rest():
                        tc.free[i] = [put_lo(j, t)]
                        res[j] = dve.op(lambda e: e.scalar_tensor_tensor(h[:, j, :], h[:, j, :], colv("fin_g", j),
                                                                         r1b, ALU.mult, ALU.mult),
                                        rs["r1b"], *rs["h_read"])

                    later.extend((gate, rest))

            res = {}
            r1b = scratch(SCR - T, T)

            def double_b():
                b, ps = bank()
                tok = mm(ps, one[:, :], dg4[:, :, :].rearrange("p a b -> p (a b)"), True, True, inc=True,
                         toks=(rs["dg"],))
                rs["r1b"] = dve.op(lambda e: e.tensor_copy(r1b, ps[:, 0:T]), tok)
                t = dve.op(lambda e: e.tensor_copy(rbc[:, :], ps[:, T:2 * T]), *rs["used"])
                rs["used"] = []
                free_bank(b, t)
                rs["t"] = dve.op(lambda e: e.tensor_tensor(rb2[:, :], rbc[:, :], rbc[:, :], ALU.mult), t)
                return True

            product(KD, [2, 1] * KD, xh, xl, x_tok, evac, {24: double_a, 48: double_b})
            OutProduct(range(KD), 3, gain_of("ffn2_g", 0)).finish()

        def attention():
            o = [0]

            def take(n):
                o[0] += n
                return scr[:, o[0] - n:o[0]]

            qn = take(2 * D).rearrange("p (a b) -> p a b", a=2)
            kv = take(1024).rearrange("p (a b) -> p a b", a=2)
            kd = take(1024).rearrange("p (a b) -> p a b", a=2)
            qT = take(8 * T).rearrange("p (a b) -> p a b", a=8)
            kT = take(4 * T).rearrange("p (a b) -> p a b", a=4)
            sc = [take(2 * 386).rearrange("p (a b) -> p a b", a=2) for _ in range(2)]
            sc.append(kd.rearrange("p a b -> p (a b)")[:, 0:772].rearrange("p (a b) -> p a b", a=2))
            pT = [take(768).rearrange("p (a b) -> p a b", a=2) for _ in range(2)]
            small = [take(8) for _ in range(3)]
            qg = take(1)
            r1 = take(32)
            r2 = take(32)
            start = f_tok[KF - 1][1]
            qg_t = dve.op(lambda e: e.tensor_scalar(qg, colv("q_g", 0), 0.125, None, ALU.mult), col_in, start)

            def project(middle=None):
                bs = [bank(), bank()]
                for k in range(KD):
                    if middle and k in middle:
                        middle[k]()
                    wt = Stream.take(4)
                    for i in range(2):
                        tok = mm3(bs[i][1], wt, xh[:, k, i * P:(i + 1) * P], xl[:, k, i * P:(i + 1) * P], x_tok[k],
                                  k == 0, k == KD - 1, False, end=(i == 1 and wt[3]))
                return bs, tok

            kvb, kv_mm = project()
            rms_a(diagonals=False)
            kvt = []
            for i in range(2):
                a = dve.op(lambda e, i=i: e.tensor_scalar(kv[:, i, :], kvb[i][1], st[:, 1, i:i + 1], None, ALU.mult),
                           kv_mm, rs["pow"])
                free_bank(kvb[i][0], a)
                kvt.append(a)

            def heads(ap):
                return ap.rearrange("p (a b) -> p a b", b=64)

            def head_norm(src, n, tok, r, sqb, dst):
                a = act.op(lambda e: e.activation(sqb, src, ACT.Square), *tok)
                c = dve.op(lambda e: e.tensor_reduce(r[:, 0:n], sqb, AX.X, ALU.add), a)
                d = dve.op(lambda e: e.tensor_scalar(r[:, 0:n], r[:, 0:n], 1.0 / 64, EPS, ALU.mult, ALU.add), c)
                f = pool.op(lambda e: e.tensor_tensor(r[:, n:2 * n], r[:, 0:n], mh[:, 0:n], ALU.pow), d)
                for out_ in dst:
                    g = dve.op(lambda e, out_=out_: e.tensor_tensor(out_, src, stretch(r[:, n:2 * n], 2, 64), ALU.mult), f)
                return g

            sqb = [take(512) for _ in range(2)]
            assert o[0] <= SCR, o[0]
            kd_t = []
            for i in range(2):
                twice = [kd[:, i, 0:512].rearrange("p (g j d) -> p g j d", j=2, d=64)[:, :, j, :] for j in range(2)]
                kd_t.append(head_norm(heads(kv[:, i, 0:256]), 4, (kvt[i],), r1[:, 8 * i:8 * i + 8],
                                      heads(sqb[i][:, 0:256]), twice))

            kT_t, qT_t, q_done = [], [], {}

            def k_transposes():
                for half in range(2):
                    b, ps = bank()
                    for g in range(2):
                        for i in range(2):
                            gg = 2 * half + g
                            tok = pe.op(lambda e, g=g, gg=gg, i=i, ps=ps: e.transpose(
                                ps[:, (2 * g + i) * P:(2 * g + i + 1) * P], kd[:, i, gg * P:(gg + 1) * P], ident),
                                *kd_t)
                    a = act.op(lambda e, half=half, ps=ps: e.activation(
                        kT[:, 2 * half:2 * half + 2, :], ps.rearrange("p (a b) -> p a b", a=2), ACT.Copy,
                        scale=colv("k_g", 0)), tok)
                    free_bank(b, a)
                    kT_t.append(a)

            def q_transposes(t):
                b, ps = bank()
                for g in range(2):
                    for i in range(2):
                        tt = 2 * t + g
                        tok = pe.op(lambda e, g=g, i=i, tt=tt: e.transpose(
                            ps[:, (2 * g + i) * P:(2 * g + i + 1) * P], qn[:, i, tt * P:(tt + 1) * P], ident),
                            q_done[t // 2, i])
                a = act.op(lambda e: e.activation(
                    qT[:, 2 * t:2 * t + 2, :], ps.rearrange("p (a b) -> p a b", a=2), ACT.Copy, scale=qg), tok, qg_t)
                free_bank(b, a)
                qT_t.append(a)

            def q_scale(c, qb, q_mm):
                toks = []
                for i in range(2):
                    dst = qn[:, i, c * 512:(c + 1) * 512]
                    a = dve.op(lambda e, dst=dst, i=i: e.tensor_scalar(dst, qb[i][1], st[:, 1, i:i + 1], None, ALU.mult), q_mm)
                    free_bank(qb[i][0], a)
                    toks.append(a)
                return toks

            def q_norm(c, i, tok):
                sq_free = (kd_t[i],) if c == 0 else (q_done[0, i],)
                src = heads(qn[:, i, c * 512:(c + 1) * 512])
                q_done[c, i] = head_norm(src, 8, (tok, *sq_free), r2[:, 16 * i:16 * i + 16], heads(sqb[i]), [src])

            q0 = q_scale(0, *project())
            for i in range(2):
                q_norm(0, i, q0[i])

            negd = cst[:, C_NEG:C_NEG + 384]
            sunk, exps, normed, pTt, val_bank = {}, {}, {}, {}, {}
            sc_free, pT_free, small_free = [[], [], kT_t], [[], []], [[], [], []]

            def put_sinks(p):
                s = sc[p % 3]
                both = row[:, 2 * p:2 * p + 2]
                sunk[p] = pool.op(lambda e: e.tensor_copy(s[:, :, 0:386:385], stretch(both, 2, 2)), row_in, start,
                                  *sc_free[p % 3])

            sc_bank = {}

            def scores(p):
                g = p // 2
                bs = [bank(), bank()]
                for part in range(2):
                    for odd in range(2):
                        r = slice(64 * odd, 64 * odd + 64)
                        ps = bs[odd][1]
                        dst, q_ap = (ps[:, 0:P], qT[r, p, 0:P]) if part == 0 else (ps[:, P:3 * P], qT[r, p, P:T])
                        k_ap = kT[r, g, 0:P] if part == 0 else kT[r, g, :]
                        tok = mm(dst, q_ap, k_ap, True, True, inc=True, toks=(qT_t[p // 2], kT_t[g // 2]))
                sc_bank[p] = bs, tok

            def softmax(p):
                s = sc[p % 3]
                bs, tok = sc_bank[p]
                for odd in range(2):
                    slope = float(2.0 ** (-8.0 * (2 * p + odd + 1) / 16))
                    ps = bs[odd][1]
                    a = dve.op(lambda e, odd=odd, ps=ps, slope=slope: e.scalar_tensor_tensor(s[:, odd, 1:385], negd, slope, ps[:, 0:384],
                                                                ALU.mult, ALU.add), tok, start, *sc_free[p % 3])
                    free_bank(bs[odd][0], a)
                nm, den = small[p % 3][:, 0:4], small[p % 3][:, 4:8]
                m0 = dve.op(lambda e: e.tensor_reduce(nm[:, 0:2], s[:, :, 0:129], AX.X, ALU.max), a, sunk[p],
                            *small_free[p % 3])
                m1 = dve.op(lambda e: e.tensor_reduce(nm[:, 2:4], s[:, :, 129:386], AX.X, ALU.max), a)
                m = dve.op(lambda e: e.tensor_scalar(nm, nm, -1.0, None, ALU.mult), m0, m1)
                for c in range(4):
                    part, odd = c // 2, c % 2
                    span = s[:, odd, 0:129] if part == 0 else s[:, odd, 129:386]
                    x = act.op(lambda e, c=c, span=span: e.activation(span, span, ACT.Exp, bias=nm[:, c:c + 1],
                                                      accum_out=den[:, c:c + 1]), m)
                exps[p] = x

            def divide(p):
                s = sc[p % 3]
                den = small[p % 3][:, 4:8]
                a = dve.op(lambda e: e.reciprocal(den, den), exps[p])
                for c in range(4):
                    part, odd = c // 2, c % 2
                    span = s[:, odd, 1:129] if part == 0 else s[:, odd, 129:385]
                    x = dve.op(lambda e, c=c, span=span: e.tensor_scalar(span, span, den[:, c:c + 1], None, ALU.mult), a)
                small_free[p % 3] = [x]
                normed[p] = x

            def weigh(p):
                s = sc[p % 3]
                toks = []
                for odd in range(2):
                    b, ps = bank()
                    for part in range(3):
                        src = s[:, odd, 1 + part * P:1 + (part + 1) * P]
                        tok = pe.op(lambda e, part=part, ps=ps, src=src: e.transpose(ps[:, part * P:(part + 1) * P], src, ident), normed[p],
                                    cst_in)
                    dst = pT[p % 2][:, odd, :]
                    if odd:
                        a = dve.op(lambda e, dst=dst, ps=ps: e.tensor_copy(dst, ps[:, 0:384]), tok, *pT_free[p % 2])
                    else:
                        a = act.op(lambda e, dst=dst, ps=ps: e.activation(dst, ps[:, 0:384], ACT.Copy), tok, *pT_free[p % 2])
                    free_bank(b, a)
                    toks.append(a)
                sc_free[p % 3] = [tok]
                pTt[p] = toks

            def values(p):
                g = p // 2
                vs = [kv[:, m_, 256 + 64 * g:256 + 64 * g + 64] for m_ in range(2)]
                b, ps = bank()
                pr = [pT[p % 2][:, :, k * P:(k + 1) * P] for k in range(3)]
                two = [ps[0:64, k * T:(k + 1) * T].rearrange("p (a b) -> p a b", a=2) for k in range(2)]
                mm(two[0], vs[0], pr[0], True, True, toks=(*pTt[p], *kvt))
                mm(two[1], vs[0], pr[1], True, False)
                tok = mm(two[1], vs[1], pr[2], False, True, inc=True)
                pT_free[p % 2] = [tok]
                val_bank[p] = b, ps, tok

            def outputs_hi(p):
                b, ps, tok = val_bank[p]
                by_head = ps[0:64, :].rearrange("p (a h b) -> p a h b", a=2, h=2)
                val_bank[p] = b, by_head
                for odd in range(2):
                    r = slice(64 * odd, 64 * odd + 64)
                    dst = fh[r, p, :].rearrange("p (a b) -> p a b", a=2)
                    a = act.op(lambda e, dst=dst, odd=odd: e.activation(dst, by_head[:, :, odd, :], ACT.Copy), tok)
                f_tok[p] = (a, None)

            def outputs_lo(p):
                b, by_head = val_bank[p]
                a = f_tok[p][0]
                for odd in range(2):
                    r = slice(64 * odd, 64 * odd + 64)
                    hi = fh[r, p, :].bitcast(F32).rearrange("p (a b) -> p a b", a=2)
                    dst = fl[r, p, :].rearrange("p (a b) -> p a b", a=2)
                    c = dve.op(lambda e, dst=dst, hi=hi, odd=odd: e.tensor_tensor(dst, by_head[:, :, odd, :], hi, ALU.subtract), a)
                free_bank(b, c)
                f_tok[p] = (a, c)

            product_out = OutProduct(range(KD), 6, gain_of("ffn2_g", 8))
            q1 = []

            def first_scores():
                q_transposes(0)
                q_transposes(1)
                scores(0)

            q1b, q1_mm = project({5: k_transposes, 7: first_scores})
            put_sinks(0)
            put_sinks(1)
            put_sinks(2)
            softmax(0)
            q1 = q_scale(1, q1b, q1_mm)
            rs["st"] = [q1[1]]
            scores(1)
            q_norm(1, 0, q1[0])
            softmax(1)
            q_norm(1, 1, q1[1])
            divide(0)
            for p in range(8):
                weigh(p)
                if p < 6:
                    scores(p + 2)
                if p < 5:
                    put_sinks(p + 3)
                if p >= 2:
                    product_out.outer(4)
                values(p)
                outputs_hi(p)
                if p < 7:
                    divide(p + 1)
                if p == 1:
                    q_transposes(2)
                if p == 2:
                    q_transposes(3)
                if p < 6:
                    softmax(p + 2)
                if p >= 2:
                    product_out.outer(4)
                outputs_lo(p)
            product_out.finish()

        load_chunk(1)
        load_chunk(2)
        for k in range(KD):
            prep(k, gain_of("mix_g", 0), (x_in[k // 4],), False)
            if k % 4 == 3:
                split_hi(k // 4)
                split_lo(k // 4)
        drain()
        for p in range(2, RING - 1):
            split_hi(p)
            split_lo(p)
        gg_tok = dve.op(lambda e: e.tensor_tensor(gg[:, :], col[:, COLS["fin_g"]:COLS["fin_g"] + KD],
                                                  col[:, COLS["mix2_g"]:COLS["mix2_g"] + KD], ALU.mult), col_in)
        act.wait(gg_tok)
        retention()
        ffn(gain_of("mix_g", 8))
        conformer()
        ffn(lambda k: gg[:, k:k + 1], squares=gain_of("fin_g", 0))
        short_conv()
        ffn(gain_of("mix2_g", 8))
        attention()
        ffn(None)
        sp.wait((s_out, 16 * KD))
        assert Stream.g == 8 * n_pieces

        block = ctx.enter_context(nc.Block())

        @block.sync
        def _(e):
            sp.play(e)

        @block.gpsimd
        def _(e):
            pool.play(e)

        @block.scalar
        def _(e):
            act.play(e)

        @block.vector
        def _(e):
            dve.play(e)

        @block.tensor
        def _(e):
            pe.play(e)


def kernel(**inputs):
    import numpy as _np
    import concourse.bacc as _bacc
    from concourse import mybir as _mybir
    from concourse.bass_utils import run_bass_kernel_spmd as _run

    a = {k: _np.asarray(v) for k, v in inputs.items()}

    def tiles(w):
        k, n = w.shape
        return w.reshape(k // 128, 128, n // 128, 128).transpose(1, 2, 0, 3)

    def strips(w):
        k, n = w.shape
        return w.reshape(k // 128, 128, n // 512, 512).transpose(1, 2, 0, 3)

    def flat(t):
        return t.reshape(128, -1)

    def wide(t, n):
        return _np.concatenate([flat(t[:, 0:n].transpose(0, 2, 1, 3)), flat(t[:, n:])], axis=1)

    def outer(w, order, n):
        t = tiles(w)[:, :, list(order), :]
        return _np.concatenate([flat(t[:, :, 0:n].transpose(0, 2, 1, 3)), flat(t[:, :, n:])], axis=1)

    def mixed(*parts):
        t = _np.stack(parts, axis=2)
        return t.reshape(128, -1, *t.shape[3:])

    w_in = a["ret_w_in"][0]
    c_in = a["conv_w_in_2"][0]
    qkv = a["attn_w_qkv_2"][0]
    pw1 = a["conv_w_pw1"][0]
    gu2 = a["ffn_w_gate_up_2"]

    def ffn(gate, up, down):
        return [wide(mixed(tiles(gate), tiles(up)), 2 * WIDE), flat(tiles(down))]

    parts = [flat(tiles(w_in[:, 0:1024])), flat(strips(w_in[:, 1024:1536])), flat(tiles(w_in[:, 2048:2560])),
             flat(tiles(w_in[:, 1536:2048])), outer(a["mix_w_out"][0], (4, 5, 6, 7, 0, 1, 2, 3), 4)]
    parts += ffn(a["ffn_w_gate"][0], a["ffn_w_up"][0], a["ffn_w_down"][0])
    parts += [flat(mixed(tiles(pw1[:, 0:1024]), tiles(pw1[:, 1024:2048]))), outer(a["conv_w_pw2"][0], range(8), 3)]
    parts += ffn(a["ffn_w_gate"][1], a["ffn_w_up"][1], a["ffn_w_down"][1])
    parts += [flat(mixed(tiles(c_in[:, 0:1024]), tiles(c_in[:, 2048:3072]), tiles(c_in[:, 1024:2048]))),
              outer(a["conv_w_out_2"][0], range(8), 3)]
    parts += ffn(gu2[0][:, 0:2816], gu2[0][:, 2816:], a["ffn_w_down_2"][0])
    parts += [flat(strips(qkv[:, 1024:1536])), flat(strips(qkv[:, 0:1024])), outer(a["attn_w_o_2"][0], range(8), 6)]
    parts += ffn(gu2[1][:, 0:2816], gu2[1][:, 2816:], a["ffn_w_down_2"][1])
    w = _np.concatenate(parts, axis=1)
    w = _np.ascontiguousarray(w.reshape(128, -1, CHUNK).transpose(1, 0, 2))

    def column(v):
        return _np.asarray(v).reshape(-1, 128).T

    cols = _np.ascontiguousarray(_np.concatenate([
        column(a["mixer_norm_g"]), column(a["ffn_norm_g"]), column(a["final_norm_g"]), column(a["ret_norm_g"]),
        column(a["pool_scale"]), column(a["conv_b_pw1"]), column(a["conv_w_dw"][0]), column(a["conv_b_dw"]),
        column(a["conv_ln_g"]), column(a["conv_ln_b"]), column(a["conv_b_pw2"]), column(a["conv_w_2"][0]),
        column(a["norm_mixer_2"]), column(a["norm_ffn_2"]),
        _np.tile(a["attn_q_gain_2"].T, (2, 1)), _np.tile(a["attn_k_gain_2"].T, (2, 1))], axis=1))
    rows = _np.ascontiguousarray(_np.broadcast_to(a["attn_sinks_2"], (128, NROW)))
    pos = _np.ascontiguousarray(_np.broadcast_to(a["positions"].reshape(1, 256), (128, 256)))
    xT = _np.ascontiguousarray(a["x"][0].T.reshape(8, 128, 256).transpose(1, 0, 2))
    poolw = _np.ascontiguousarray(a["pool_w"][0].transpose(1, 0, 2))

    c = _np.zeros((128, NCONST), _np.float32)
    c[:, C_ID:C_ID + 128] = _np.eye(128)
    i = _np.arange(128)[:, None]
    j = _np.arange(256)[None, :]
    for hd in range(4):
        lg = _np.log1p(-(2.0 ** (-5.0 - hd)))
        c[:, C_DEC + 256 * hd:C_DEC + 256 * hd + 256] = _np.where(
            j >= i, _np.exp(lg * _np.maximum(j - i, 0)), 0.0) * 128.0 ** -0.5
    dist = i + 128 - j
    far = _np.where((dist >= 0) & (dist < 128), -dist, -1e33)
    c[:, C_NEG:C_NEG + 384] = _np.concatenate([far[:, 128:256], far], axis=1)
    for g in range(4):
        wnd = 2 << g
        c[:, C_COR + 16 * g:C_COR + 16 * g + 16] = wnd / _np.minimum(_np.arange(16) + 1, wnd)
    f = _np.float32(10000.0) ** (-_np.arange(64, dtype=_np.float32) / _np.float32(64))
    c[:, C_INV] = _np.concatenate([f, f])
    c[0:64, C_SGN] = 1.0
    c[64:128, C_SGN] = -1.0

    nc = _bacc.Bacc("TRN2", target_bir_lowering=False, num_devices=1)
    arrays = {"w": w, "poolw": poolw, "xT": xT, "pos": pos, "cols": cols, "rows": rows, "consts": c}
    aps = [nc.dram_tensor(n, v.shape, _mybir.dt.from_np(v.dtype), kind="ExternalInput").ap()
           for n, v in arrays.items()]
    out = nc.dram_tensor("out", (128, 8, 256), _mybir.dt.float32, kind="ExternalOutput").ap()
    model_kernel(nc, *aps, out)
    r = _run(nc, [arrays], core_ids=[0])
    got = _np.asarray(r.results[0]["out"])
    return _np.ascontiguousarray(got.transpose(1, 0, 2).reshape(1024, 256).T)[None]
```

```python
from contextlib import ExitStack

import numpy as np
import concourse.bass as bass
from concourse import mybir

F32 = mybir.dt.float32
F32R = mybir.dt.float32r
I32 = mybir.dt.int32
ALU = mybir.AluOpType
ACT = mybir.ActivationFunctionType
AX = mybir.AxisListType

P = 128
D = 1024
T = 256
KD = D // P
FF = 2816
KF = FF // P
EPS = 1e-6
PIECE = 1024
CHUNK = 2 * PIECE
RAW = 3
RING = 6
SCR = 12032
TAPS = (13, 13, 13, 13, 13, 13, 16, 18)
WIDE = 2
SQUARES = 3
WARM_START = 14
N_RET = 5
N_CONF = 4
N_SHORT = 4
N_ATT = 6
DIAGS = 24

COLS = {}
_at = 0
for _name, _n in (("mix_g", 16), ("inv", 1), ("sgn", 1), ("ffn_g", 16), ("fin_g", 8), ("ret_g", 4), ("pool_s", 4), ("b_pw1", 16),
                  ("w_dw", 31 * 8), ("b_dw", 8), ("ln_g", 8), ("ln_b", 8), ("b_pw2", 8), ("w_c3", 24),
                  ("mix2_g", 16), ("ffn2_g", 16), ("q_g", 1), ("k_g", 1)):
    COLS[_name] = _at
    _at += _n
NCOL = _at
FIRST_COLS = 18
C_ID, C_DEC, C_NEG, C_COR = 0, 128, 128 + 1024, 1536
NCONST = 1600
NROW = 16

TWO_PI = 2.0 * np.pi
P1 = 6.28125
P2 = float(np.float32(np.round((TWO_PI - P1) * 2.0**17) / 2.0**17))
P3 = float(np.float32(np.round((TWO_PI - P1 - P2) * 2.0**27) / 2.0**27))
P4 = float(np.float32(TWO_PI - P1 - P2 - P3))
MAGIC = 1.5 * 2.0**23
HALF_PI = float(np.float32(np.pi / 2))
PI_IN = 3.1415925


class Queue:

    def __init__(self, sem):
        self.sem, self.n, self.items, self.seen = sem, 0, [], {}

    def wait(self, *toks):
        for sem, val in toks:
            if self.seen.get(id(sem), 0) < val:
                self.seen[id(sem)] = val
                self.items.append(lambda e, s=sem, v=val: e.wait_ge(s, v))

    def op(self, fn, *toks):
        self.wait(*toks)
        self.n += 1
        self.items.append(lambda e: fn(e).then_inc(self.sem, 1))
        return (self.sem, self.n)

    def raw(self, fn, *toks):
        self.wait(*toks)
        self.items.append(lambda e: fn(e))

    def play(self, e):
        for item in self.items:
            item(e)


class Slots:

    def __init__(self, aps):
        self.aps, self.free, self.i = aps, [[] for _ in aps], -1

    def next(self):
        self.i += 1
        k = self.i % len(self.aps)
        return k, self.aps[k], self.free[k]


def stretch(ap, axis, n):
    shape = list(ap.shape)
    shape.insert(axis, n)
    return ap.unsqueeze(axis).broadcast_to(shape)


def model_kernel(nc, w, poolw, xT, pos, cols, rows, consts, out):
    ctx = ExitStack()
    with ctx:
        def sb(name, shape, dt=F32):
            return ctx.enter_context(nc.sbuf_tensor(name, shape, dt))

        def sem(name):
            return ctx.enter_context(nc.semaphore(name))

        raw_t = sb("raw_t", [P, RAW, CHUNK])
        hi_t = sb("hi_t", [P, RING, PIECE], F32R)
        lo_t = sb("lo_t", [P, RING, PIECE], F32R)
        h = sb("h", [P, KD, T])
        xh = sb("xh", [P, KD, T], F32R)
        xl = sb("xl", [P, KD, T], F32R)
        fh = sb("fh", [P, KF, T], F32R)
        fl = sb("fl", [P, KF, T], F32R)
        cst = sb("cst", [P, NCONST])
        col = sb("col", [P, NCOL])
        row = sb("row", [P, NROW])
        pw = sb("pw", [P, 4, P])
        one = sb("one", [P, P])
        mh = sb("mh", [P, 32])
        rbc = sb("rbc", [P, T])
        rb2 = sb("rb2", [P, T])
        ssum = sb("ssum", [P, T])
        sq = sb("sq", [P, 2, T])
        dg4 = sb("dg", [P, 4, P])
        dg = dg4[:, 0:2, :]
        st = sb("st", [P, 6, 2])
        ssum2 = sb("ssum2", [P, T])
        gg = sb("gg", [P, KD])
        scr = sb("scr", [P, SCR])
        banks = ctx.enter_context(nc.psum_tensor("banks", [P, 8, 512], F32))
        ident = cst[:, C_ID:C_ID + P]

        pe = Queue(sem("s_pe"))
        dve = Queue(sem("s_dve"))
        act = Queue(sem("s_act"))
        pool = Queue(sem("s_pool"))
        sp = Queue(sem("s_sp"))
        s_raw = [sem(f"s_raw{i}") for i in range(RAW)]
        s_ld = {n: sem("s_ld_" + n) for n in ("x0", "x1", "cst", "col", "col0", "row", "pw", "pos")}
        s_first = sem("s_first")
        s_out = sem("s_out")

        def colv(name, i):
            return col[:, COLS[name] + i:COLS[name] + i + 1]

        def load(q, name, dst, src):
            q.raw(lambda e: e.dma_start(dst, src).then_inc(s_ld[name], 16))
            return (s_ld[name], 16)

        col0_in = load(act, "col0", col[:, 0:FIRST_COLS], cols[:, 0:FIRST_COLS])
        pos_in = load(act, "pos", scr[:, 0:T].bitcast(I32), pos)
        x_in = [load(sp, "x0", h[:, 0:2, :], xT[:, 0:2, :])]
        sp.raw(lambda e: e.dma_start(raw_t[:, 0, 0:PIECE], w[0, :, 0:PIECE]).then_inc(s_first, 16))
        x_in.append(load(sp, "x1", h[:, 2:8, :], xT[:, 2:8, :]))
        sp.raw(lambda e: e.dma_start(raw_t[:, 0, PIECE:CHUNK], w[0, :, PIECE:CHUNK]).then_inc(s_raw[0], 16))
        posi = scr[:, 0:T].bitcast(I32)
        col_in = load(sp, "col", col[:, FIRST_COLS:NCOL], cols[:, FIRST_COLS:NCOL])

        n_pieces = w.shape[0] * 2
        hi_tok, lo_tok, freed = {}, {}, {}

        def load_chunk(c):
            if c >= w.shape[0]:
                return
            if c >= RAW:
                for p in (2 * (c - RAW), 2 * (c - RAW) + 1):
                    sp.wait(hi_tok[p], lo_tok[p])
            sp.raw(lambda e: e.dma_start(raw_t[:, c % RAW, :], w[c]).then_inc(s_raw[c % RAW], 16))

        def arrived(p):
            return (s_first, 16) if p == 0 else (s_raw[p // 2 % RAW], 16 * (p // 2 // RAW + 1))

        def slot_free(p):
            return [freed[p - RING]] if p >= RING else []

        def raw_of(p):
            return raw_t[:, p // 2 % RAW, (p % 2) * PIECE:(p % 2 + 1) * PIECE]

        def split_hi(p):
            hi_tok[p] = act.op(lambda e: e.activation(hi_t[:, p % RING, :], raw_of(p), ACT.Copy), arrived(p),
                               *slot_free(p))

        def split_lo(p):
            lo_tok[p] = dve.op(lambda e: e.tensor_tensor(lo_t[:, p % RING, :], raw_of(p),
                                                         hi_t[:, p % RING, :].bitcast(F32), ALU.subtract),
                               arrived(p), *slot_free(p), hi_tok[p])
            if p % 2:
                load_chunk(p // 2 + RAW)

        class Stream:
            g = 0
            flushed = 0

            @classmethod
            def take(cls, n):
                p, r = cls.g // 8, cls.g % 8
                cls.g += n
                if r >= 3 and cls.flushed < p:
                    cls.flushed = p
                    flush()
                s = slice(r * P, (r + n) * P)
                return p, hi_t[:, p % RING, s], lo_t[:, p % RING, s], (r + n == 8)

        pending, lo_next, later, sums_due = [], [], [], []

        def release(p, tok):
            freed[p] = tok
            if p - 1 + RING < n_pieces:
                pending.append(p - 1 + RING)

        def flush():
            while pending:
                split_hi(pending[0])
                if lo_next:
                    split_lo(lo_next.pop(0))
                lo_next.append(pending.pop(0))
            if len(freed) >= n_pieces - RING:
                while lo_next:
                    split_lo(lo_next.pop(0))
            if later:
                later.pop(0)()
            for _ in range(SQUARES):
                if sums_due:
                    sums_due.pop(0)()

        def drain():
            while later:
                later.pop(0)()

        def drain_squares():
            drain()
            while sums_due:
                sums_due.pop(0)()

        def keep_warm(n):
            b, ps = bank()
            for _ in range(n):
                mm(ps[:, 0:P], one[:, :], one[:, :], True, True, toks=(ones_tok,))
            idle.append(b)

        bank_free = [[] for _ in range(8)]
        idle = list(range(8))

        def bank():
            b = idle.pop(0)
            pe.wait(*bank_free[b])
            return b, banks[:, b, :]

        def free_bank(b, *toks):
            bank_free[b] = list(toks)
            idle.append(b)

        def mm(out_, l, r_, start, stop, inc=False, toks=(), skip=False):
            fn = lambda e: e.matmul(out_, l, r_, start=start, stop=stop, skip_group_check=skip)
            if inc:
                return pe.op(fn, *toks)
            pe.raw(fn, *toks)

        def mm3(out_, wt, a_hi, a_lo, toks, first, last, stationary_w, end=None, skip=False):
            p, w_hi, w_lo, ends = wt
            end = ends if end is None else end
            pairs = ((w_hi, a_hi), (w_hi, a_lo), (w_lo, a_hi))
            tok = None
            for i, (a, b) in enumerate(pairs):
                need = (hi_tok[p], toks[0]) if i == 0 else ((toks[1],) if i == 1 else (lo_tok[p],))
                l, r_ = (a, b) if stationary_w else (b, a)
                tok = mm(out_, l, r_, first and i == 0, last and i == 2, inc=(i == 2 and (end or last)), toks=need, skip=skip)
            if end:
                release(p, tok)
            return tok

        def product(nk, units, a_hi, a_lo, a_tok, evac, hooks=None, wide=1):
            hooks = dict(hooks or {})
            late, count = [], 0
            ready = not hooks
            for u in [0] + list(range(wide, len(units))):
                group = list(range(u, u + (wide if u == 0 else 1)))
                open_banks = [bank() for _ in group]
                one_k = [(ps, t) for (b, ps), v in zip(open_banks, group) for t in range(units[v])]
                if u == 0 and wide > 1:
                    order = [(k, ps, t) for k in range(nk) for ps, t in one_k]
                else:
                    order = [(k, ps, t) for ps, t in one_k for k in range(nk)]
                toks = {}
                for k, ps, t in order:
                    if a_tok[k] is None or a_tok[k][1] is None:
                        drain()
                    wt = Stream.take(1)
                    tok = mm3(ps[:, t * T:(t + 1) * T], wt, a_hi[:, k, :], a_lo[:, k, :], a_tok[k],
                              k == 0 and (wide == 1 or u > 0 or t == 0), k == nk - 1, True, skip=wide > 1)
                    count += 1
                    if count in hooks:
                        ready = hooks.pop(count)() or ready
                        if ready:
                            for item in late:
                                evac(*item)
                            late = []
                    if k == nk - 1:
                        toks[id(ps)] = tok
                for v, (b, ps) in zip(group, open_banks):
                    late.append((v, b, ps, toks[id(ps)]))
                if ready:
                    for item in late:
                        evac(*item)
                    late = []
            assert not late and not hooks

        ones_tok = dve.op(lambda e: e.memset(one[:, :], 1.0))
        mh_tok = pool.op(lambda e: e.memset(mh[:, :], -0.5))
        x_tok = [None] * KD
        ss = {}

        sqs = Slots([sq[:, 0, :], sq[:, 1, :]])

        def prep(k, gain, src_tok, put_off, squares=None):
            x_tok[k] = None
            a = act.op(lambda e: e.activation(xh[:, k, :], h[:, k, :], ACT.Copy, scale=gain(k)), *src_tok)

            def lo():
                b = dve.op(lambda e: e.scalar_tensor_tensor(xl[:, k, :], h[:, k, :], gain(k),
                                                            xh[:, k, :].bitcast(F32), ALU.mult, ALU.subtract), a)
                x_tok[k] = (a, b)

            def square():
                one_square(k, ssum, "t", src_tok, None)
                if squares:
                    one_square(k, ssum2, "t2", src_tok, squares)

            if put_off is None:
                lo()
            else:
                put_off.append(lo)
            sums_due.append(square)

        def one_square(k, dst, key, src_tok, scale):
            by = {} if scale is None else {"scale": scale(k)}
            if k == 0:
                ss[key] = act.op(lambda e: e.activation(dst[:, :], h[:, 0, :], ACT.Square, **by), *src_tok,
                                 *ss.get("read", []))
            else:
                i, buf, free = sqs.next()
                s = act.op(lambda e: e.activation(buf, h[:, k, :], ACT.Square, **by), *src_tok, *free)
                ss[key] = dve.op(lambda e: e.tensor_tensor(dst[:, :], dst[:, :], buf, ALU.add), s, ss[key])
                sqs.free[i] = [ss[key]]

        def gain_of(name, first):
            return lambda k: colv(name, first + k)

        rs = {"used": [], "st": []}

        def rms_a(diagonals=True):
            drain_squares()
            b, ps = bank()
            for i in range(2):
                tok = mm(ps[:, i:i + 1], ssum[:, i * P:(i + 1) * P], one[:, 0:1], True, True, inc=True,
                         toks=(ss["t"], ones_tok))
            ss["read"] = [tok]
            a = dve.op(lambda e: e.tensor_scalar(st[:, 0, :], ps[:, 0:2], 1.0 / D, EPS, ALU.mult, ALU.add), tok)
            free_bank(b, a)
            c = pool.op(lambda e: e.tensor_tensor(st[:, 1, :], st[:, 0, :], mh[:, 0:2], ALU.pow), a, mh_tok,
                        *rs["st"])
            rs["st"] = []
            rs["pow"] = c
            for i in range(2 if diagonals else 0):
                rs["dg"] = dve.op(lambda e, i=i: e.tensor_scalar(dg[:, i, :], ident, st[:, 1, i:i + 1], None, ALU.mult),
                                  c, cst_in)

        def rms_b(square=False):
            b, ps = bank()
            tok = mm(ps[:, 0:T], one[:, :], dg[:, :, :].rearrange("p a b -> p (a b)"), True, True, inc=True,
                     toks=(rs["dg"],))
            rs["t"] = dve.op(lambda e: e.tensor_copy(rbc[:, :], ps[:, 0:T]), tok, *rs["used"])
            free_bank(b, rs["t"])
            rs["used"] = []
            if square:
                rs["t"] = dve.op(lambda e: e.tensor_tensor(rb2[:, :], rbc[:, :], rbc[:, :], ALU.mult), rs["t"])

        def double_a():
            drain_squares()
            b, ps = bank()
            for n, sums in enumerate((ssum, ssum2)):
                for i in range(2):
                    tok = mm(ps[:, 2 * n + i:2 * n + i + 1], sums[:, i * P:(i + 1) * P], one[:, 0:1], True, True,
                             inc=True, toks=(ss["t"], ss["t2"]))
            ss["read"] = [tok]
            rs["h_read"] = [ss["t"], ss["t2"], x_tok[KD - 1][1]]
            a = dve.op(lambda e: e.tensor_scalar(st[:, 0, :], ps[:, 0:2], 1.0 / D, EPS, ALU.mult, ALU.add), tok,
                       rs["pow"])
            m2 = dve.op(lambda e: e.tensor_scalar(st[:, 2, :], ps[:, 2:4], 1.0 / D, None, ALU.mult))
            free_bank(b, m2)
            r1 = pool.op(lambda e: e.tensor_tensor(st[:, 3, :], st[:, 0, :], mh[:, 0:2], ALU.pow), a)
            t = pool.op(lambda e: e.tensor_tensor(st[:, 4, :], st[:, 3, :], st[:, 3, :], ALU.mult), r1)
            t = pool.op(lambda e: e.tensor_tensor(st[:, 4, :], st[:, 4, :], st[:, 2, :], ALU.mult), t, m2)
            t = pool.op(lambda e: e.tensor_scalar(st[:, 4, :], st[:, 4, :], EPS, None, ALU.add), t)
            t = pool.op(lambda e: e.tensor_tensor(st[:, 5, :], st[:, 4, :], mh[:, 0:2], ALU.pow), t)
            t = pool.op(lambda e: e.tensor_tensor(st[:, 1, :], st[:, 3, :], st[:, 5, :], ALU.mult), t)
            for n in range(4):
                src = st[:, 3 if n < 2 else 1, n % 2:n % 2 + 1]
                rs["dg"] = dve.op(lambda e, n=n, src=src: e.tensor_scalar(dg4[:, n, :], ident, src, None, ALU.mult),
                                  t, cst_in, *rs.get("dg_free", []))

        def rms_hooks(a=32, b=44, extra=None):
            def last():
                rms_b()
                if extra:
                    extra()
                return True
            return {a: rms_a, b: last}

        def scratch(off, n):
            return scr[:, off:off + n]

        f_tok = [None] * KF

        def put_hi(k, src, tok):
            f_tok[k] = (act.op(lambda e: e.activation(fh[:, k, :], src, ACT.Copy), tok), None)

        def put_lo(k, src):
            a = f_tok[k][0]
            f_tok[k] = (a, dve.op(lambda e: e.tensor_tensor(fl[:, k, :], src, fh[:, k, :].bitcast(F32),
                                                            ALU.subtract), a))
            return f_tok[k][1]

        def put_f(k, src, toks, n=1):
            a = act.op(lambda e: e.activation(fh[:, k:k + n, :], src, ACT.Copy), *toks)
            b = dve.op(lambda e: e.tensor_tensor(fl[:, k:k + n, :], src, fh[:, k:k + n, :].bitcast(F32),
                                                 ALU.subtract), a)
            for i in range(n):
                f_tok[k + i] = (a, b)
            return b

        def ffn(next_gain, squares=None):
            t_ring = Slots([scratch(i * 512, 512) for i in range(3)])
            s_ring = Slots([scratch(1536 + i * T, T) for i in range(2)])
            m_ring = Slots([scratch(2048 + i * T, T) for i in range(2)])
            begun, ended = [], [0]

            def up(u, b, ps, tok):
                f_tok[u] = None
                while len(begun) > ended[0] + 1:
                    later.pop(0)()
                begun.append(u)
                i, t, free = t_ring.next()
                j, s, sfree = s_ring.next()
                l, m, mfree = m_ring.next()
                tv = t.rearrange("p (a b) -> p a b", a=2)
                a = dve.op(lambda e: e.tensor_tensor(tv, ps.rearrange("p (a b) -> p a b", a=2),
                                                     stretch(rbc[:, :], 1, 2), ALU.mult), tok, rs["t"], *free)
                free_bank(b, a)
                rs["used"] = [a]
                c = act.op(lambda e: e.activation(s, t[:, 0:T], ACT.Silu), a, *sfree)

                def gate():
                    d = dve.op(lambda e: e.tensor_tensor(m, s, t[:, T:2 * T], ALU.mult), c, *mfree)
                    t_ring.free[i] = s_ring.free[j] = [d]
                    put_hi(u, m, d)

                def rest():
                    m_ring.free[l] = [put_lo(u, m)]
                    ended[0] += 1

                later.extend((gate, rest))

            product(KD, [2] * KF, xh, xl, x_tok, up, rms_hooks(), wide=WIDE)

            def down(u, b, ps, tok):
                a = dve.op(lambda e: e.tensor_tensor(h[:, u, :], ps[:, 0:T], h[:, u, :], ALU.add), tok)
                free_bank(b, a)
                if next_gain:
                    prep(u, next_gain, (a,), later if u < 7 else None, squares)
                else:
                    sp.raw(lambda e: e.dma_start(out[:, u, :], h[:, u, :]).then_inc(s_out, 16), a)

            product(KF, [1] * KD, fh, fl, f_tok, down)

        class OutProduct:

            def __init__(self, order, n_outer, next_gain, bias=None):
                self.order, self.n_outer = order, n_outer
                self.next_gain, self.bias = next_gain, bias
                self.banks, self.done, self.at = None, 0, 0

            def block(self, j, n):
                if self.banks is None:
                    self.banks = [bank() for _ in range(4)]
                    drain()
                k = self.order[n]
                wt = Stream.take(1)
                ps = self.banks[j // 2][1][:, (j % 2) * T:(j % 2 + 1) * T]
                return mm3(ps, wt, fh[:, k, :], fl[:, k, :], f_tok[k], n == 0 and j % 2 == 0, n == KD - 1, True,
                           skip=True)

            def outer(self, blocks=8):
                for _ in range(blocks):
                    self.block(self.at, self.done)
                    self.at += 1
                    if self.at == 8:
                        self.at, self.done = 0, self.done + 1

            def finish(self):
                while self.done < self.n_outer:
                    self.outer(8 - self.at)
                steps = []
                for pair in range(4):
                    for j in (2 * pair, 2 * pair + 1):
                        for n in range(self.n_outer, KD):
                            tok = self.block(j, n)
                    b, ps = self.banks[pair]
                    bias = self.bias
                    pair_h = h[:, 2 * pair:2 * pair + 2, :]
                    if bias is None:
                        a = dve.op(lambda e, pair_h=pair_h, ps=ps: e.tensor_tensor(pair_h, ps.rearrange("p (a b) -> p a b", a=2), pair_h,
                                                             ALU.add), tok)
                    else:
                        for j in (2 * pair, 2 * pair + 1):
                            src = ps[:, (j % 2) * T:(j % 2 + 1) * T]
                            a = dve.op(lambda e, bias=bias, j=j, src=src: e.scalar_tensor_tensor(
                                h[:, j, :], src, colv(bias, j), h[:, j, :], ALU.add, ALU.add), tok, col_in)
                    free_bank(b, a)
                    for step in steps:
                        step()
                    steps = []
                    for j in (2 * pair, 2 * pair + 1):
                        prep(j, self.next_gain, (a,), steps)
                for step in steps:
                    step()

        trig = {}
        cos, sin, w0, w1, kk = (scr[:, i * T:(i + 1) * T] for i in range(5))

        ang = w1

        def angle(fn, *toks):
            trig["t"] = dve.op(fn, *toks, *([trig["t"]] if "t" in trig else []))

        angle_steps = [
            lambda: angle(lambda e: e.tensor_copy(w0, posi), pos_in),
            lambda: angle(lambda e: e.tensor_scalar(ang, w0, colv("inv", 0), None, ALU.mult), col0_in),
            lambda: angle(lambda e: e.tensor_scalar(kk, ang, float(1 / TWO_PI), MAGIC, ALU.mult, ALU.add)),
            lambda: angle(lambda e: e.tensor_scalar(kk, kk, MAGIC, None, ALU.subtract)),
            *[lambda c=c: angle(lambda e: e.scalar_tensor_tensor(ang, kk, -c, ang, ALU.mult, ALU.add))
              for c in (P1, P2, P3, P4)],
            lambda: angle(lambda e: e.tensor_scalar(kk, ang, HALF_PI, float(-TWO_PI), ALU.is_gt, ALU.mult)),
            lambda: angle(lambda e: e.scalar_tensor_tensor(w0, ang, HALF_PI, kk, ALU.add, ALU.add)),
            lambda: angle(lambda e: e.tensor_scalar(w1, ang, PI_IN, -PI_IN, ALU.min, ALU.max)),
            lambda: angle(lambda e: e.tensor_scalar(w0, w0, PI_IN, -PI_IN, ALU.min, ALU.max))]

        def retention_sines():
            trig["sin"] = act.op(lambda e: e.activation(sin, w1, ACT.Sin, scale=colv("sgn", 0)), trig["t"])
            trig["cos"] = act.op(lambda e: e.activation(cos, w0, ACT.Sin))

        def retention():
            cosr, sinr = scratch(4 * T, T), scratch(5 * T, T)
            qk = scratch(6 * T, 8 * T).rearrange("p (a b) -> p a b", a=8)
            vt = scratch(14 * T, 4 * T).rearrange("p (a b) -> p a b", a=2)
            gs = scratch(18 * T, 4 * T).rearrange("p (a b) -> p a b", a=4)
            UP = 16 + T
            up = scratch(22 * T, 4 * UP).rearrange("p (a b) -> p a b", a=4)
            o0 = 22 * T + 4 * UP
            ta = Slots([scratch(o0 + i * 512, 512) for i in range(2)])
            tb = Slots([scratch(o0 + 1024 + i * 512, 512) for i in range(2)])
            o1 = o0 + 2048
            sT = scratch(o1, 4 * 384).rearrange("p (a b) -> p a b", a=4)
            o2 = o1 + 4 * 384
            assert o2 <= SCR
            pad_t = pool.op(lambda e: e.memset(up[:, :, 0:16], 0.0))
            rr = {}

            def tables():
                a = dve.op(lambda e: e.tensor_tensor(cosr, cos, rbc[:, :], ALU.mult), trig["cos"], rs["t"])
                rr["t"] = dve.op(lambda e: e.tensor_tensor(sinr, sin, rbc[:, :], ALU.mult), trig["sin"], a)

            qk_tok = {}

            def two(ap):
                return ap.rearrange("p (a b) -> p a b", a=2)

            def qk_evac(u, b, ps, tok):
                def swap():
                    i, a_, afree = ta.next()
                    j, b_, bfree = tb.next()
                    c = act.op(lambda e: e.activation(b_[0:64], ps[64:128], ACT.Copy), tok, *bfree)
                    c = act.op(lambda e: e.activation(b_[64:128], ps[0:64], ACT.Copy))
                    a = dve.op(lambda e: e.tensor_tensor(two(a_), two(ps), stretch(cosr, 1, 2), ALU.mult),
                               c, rr["t"], *afree)
                    free_bank(b, a)
                    c = dve.op(lambda e: e.tensor_tensor(two(b_), two(b_), stretch(sinr, 1, 2), ALU.mult))
                    d = dve.op(lambda e: e.tensor_tensor(qk[:, 2 * u:2 * u + 2, :], two(a_), two(b_), ALU.add), a, c)
                    ta.free[i] = tb.free[j] = [d]
                    qk_tok[u] = d

                later.append(swap)

            product(KD, [2] * 4, xh, xl, x_tok, qk_evac, rms_hooks(34, 46, extra=tables))

            vb = [bank(), bank()]
            for k in range(KD):
                wt = Stream.take(4)
                for i in range(2):
                    vtok = mm3(vb[i][1], wt, xh[:, k, i * P:(i + 1) * P], xl[:, k, i * P:(i + 1) * P], x_tok[k],
                               k == 0, k == KD - 1, False, end=(i == 1 and wt[3]))
            v_tok = []
            for i in range(2):
                a = dve.op(lambda e, i=i: e.tensor_scalar(vt[:, i, :], vb[i][1], st[:, 1, i:i + 1], None, ALU.mult),
                           vtok, rs["pow"])
                free_bank(vb[i][0], a)
                v_tok.append(a)
            rs["st"] = [v_tok[1]]

            drain()
            u_tok = {}

            def u_evac(u, b, ps, tok):
                a = dve.op(lambda e: e.tensor_tensor(up[:, 2 * u:2 * u + 2, 16:UP], two(ps),
                                                     stretch(rbc[:, :], 1, 2), ALU.mult), tok, rs["t"])
                free_bank(b, a)
                u_tok[u] = a

            product(KD, [2, 2], xh, xl, x_tok, u_evac)
            y_tok = []
            y_ap = [cos, sin, cosr, sinr]
            wide = Slots([scratch(o1, UP), scratch(o1 + UP, UP)])
            for gi in range(4):
                cur, t = up[:, gi, :], u_tok[gi // 2]
                n = gi + 1
                for s in range(n):
                    sh = 1 << s
                    i, dst, free = wide.next()
                    lo = 2 * sh - 1
                    t2 = pool.op(lambda e, dst=dst, cur=cur, sh=sh, lo=lo: e.tensor_tensor(
                        dst[:, lo:UP], cur[:, lo:UP], cur[:, lo - sh:UP - sh], ALU.add),
                        t, pad_t, *free)
                    cur, t = dst, t2
                    wide.free[i] = []
                t = pool.op(lambda e, cur=cur, gi=gi: e.tensor_tensor(
                    cur[:, 16:32], cur[:, 16:32], cst[:, C_COR + 16 * gi:C_COR + 16 * gi + 16], ALU.mult), t, cst_in)
                t = dve.op(lambda e, cur=cur, gi=gi: e.scalar_tensor_tensor(
                    y_ap[gi], cur[:, 16:UP], 1.0 / (2 << gi), up[:, gi, 16:UP], ALU.mult, ALU.subtract),
                    t, *qk_tok.values())
                wide.free[wide.i % 2] = [t]
                y_tok.append(t)
            wide_done = y_tok[3]

            s_tok = []
            def head_scores(hd):
                b, ps = bank()
                mm(ps[:, 0:T], qk[:, 4 + hd, 0:P], qk[:, hd, :], True, True,
                   toks=(qk_tok[hd // 2], qk_tok[2 + hd // 2]))
                tok = mm(ps[:, T:T + P], qk[:, 4 + hd, P:T], qk[:, hd, P:T], True, True, inc=True)
                dec = cst[:, C_DEC + T * hd:C_DEC + T * hd + T]
                a = dve.op(lambda e: e.tensor_tensor(sT[:, hd, 0:T], ps[:, 0:T], dec, ALU.mult),
                           tok, wide_done)
                a = dve.op(lambda e: e.tensor_tensor(sT[:, hd, T:T + P], ps[:, T:T + P],
                                                                            dec[:, 0:P], ALU.mult))
                free_bank(b, a)
                s_tok.append(a)
                return hd == 3

            gs_tok = {}

            def g_evac(u, b, ps, tok):
                i, a_, afree = ta.next()
                a = dve.op(lambda e: e.tensor_tensor(two(a_), two(ps), stretch(rbc[:, :], 1, 2), ALU.mult),
                           tok, rs["t"], *afree)
                free_bank(b, a)
                rs["used"] = [a]
                c = act.op(lambda e: e.activation(gs[:, 2 * u:2 * u + 2, :], two(a_), ACT.Silu), a)
                ta.free[i] = [c]
                gs_tok[u] = c

            product(KD, [2, 2], xh, xl, x_tok, g_evac, {4 + 8 * hd: lambda hd=hd: head_scores(hd) for hd in range(4)})

            oT = qk[:, 0:4, :]
            o2 = qk[:, 4:8, :]
            o_tok = []
            for pr in range(2):
                b, ps = bank()
                for i in range(2):
                    hd = 2 * pr + i
                    vs = [vt[:, m, hd * P:(hd + 1) * P] for m in range(2)]
                    mm(ps[:, i * T:(i + 1) * T], vs[0], sT[:, hd, 0:T], True, False, toks=(s_tok[hd], v_tok[1]))
                    tok = mm(ps[:, i * T + P:(i + 1) * T], vs[1], sT[:, hd, T:T + P], False, True, inc=True)
                a = dve.op(lambda e, pr=pr, ps=ps: e.tensor_copy(oT[:, 2 * pr:2 * pr + 2, :], two(ps)), tok)
                free_bank(b, a)
                o_tok.append(a)
            for half in range(2):
                b, ps = bank()
                for i in range(2):
                    gi = 2 * half + i
                    tok = mm(ps[:, i * T:(i + 1) * T], pw[:, gi, :], y_ap[gi], True, True, inc=True,
                             toks=(pw_in, y_tok[gi]))
                for i in range(2):
                    gi = 2 * half + i
                    a = act.op(lambda e, gi=gi, i=i, ps=ps: e.activation(
                        fh[:, 4 + gi, :], ps[:, i * T:(i + 1) * T], ACT.Copy, scale=colv("pool_s", gi)), tok, col_in)
                for i in range(2):
                    gi = 2 * half + i
                    c = dve.op(lambda e, gi=gi, i=i, ps=ps: e.scalar_tensor_tensor(
                        fl[:, 4 + gi, :], ps[:, i * T:(i + 1) * T], colv("pool_s", gi),
                        fh[:, 4 + gi, :].bitcast(F32), ALU.mult, ALU.subtract), a)
                    f_tok[4 + gi] = (a, c)
                free_bank(b, a, c)
            product_out = OutProduct((4, 5, 6, 7, 0, 1, 2, 3), N_RET, gain_of("ffn_g", 0))
            product_out.outer(4)
            sq_tok, d_tok = [], []
            for pr in range(2):
                b, ps = bank()
                tok = mm(ps, one[:, :], oT[:, 2 * pr:2 * pr + 2, :], True, True, inc=True, toks=(o_tok[pr],))
                a = dve.op(lambda e, pr=pr, ps=ps: e.scalar_tensor_tensor(
                    oT[:, 2 * pr:2 * pr + 2, :], two(ps), -1.0 / P, oT[:, 2 * pr:2 * pr + 2, :], ALU.mult, ALU.add),
                    tok)
                free_bank(b, a)
                d_tok.append(a)
                sq_tok.append(act.op(lambda e, pr=pr, o2=o2: e.activation(o2[:, 2 * pr:2 * pr + 2, :],
                                                                   oT[:, 2 * pr:2 * pr + 2, :], ACT.Square), a))
                product_out.outer(8)
            b, ps = bank()
            for hd in range(4):
                for i in range(2):
                    tok = mm(ps[:, 2 * hd + i:2 * hd + i + 1], o2[:, hd, i * P:(i + 1) * P], one[:, 0:1], True, True,
                             inc=True, toks=(sq_tok[hd // 2],))
            gst = up[:, 0, 0:16]
            a = dve.op(lambda e, ps=ps: e.tensor_scalar(gst[:, 0:8], ps[:, 0:8], 1.0 / P, EPS, ALU.mult, ALU.add), tok,
                       *y_tok)
            free_bank(b, a)
            c = pool.op(lambda e: e.tensor_tensor(gst[:, 8:16], gst[:, 0:8], mh[:, 0:8], ALU.pow), a)
            dgs = sT.rearrange("p a b -> p (a b)")
            product_out.outer(12)
            for i in range(8):
                dtok = dve.op(lambda e, i=i: e.tensor_scalar(dgs[:, i * P:(i + 1) * P], ident, gst[:, 8 + i:9 + i],
                                                             None, ALU.mult), c, tok)
            for pr in range(2):
                b, ps = bank()
                tok = mm(ps, one[:, :], dgs[:, pr * 512:(pr + 1) * 512], True, True, inc=True, toks=(dtok,))
                a = dve.op(lambda e, pr=pr, ps=ps: e.tensor_tensor(
                    oT[:, 2 * pr:2 * pr + 2, :], two(ps), oT[:, 2 * pr:2 * pr + 2, :], ALU.mult), tok,
                    sq_tok[pr])
                free_bank(b, a)
                for i in range(2):
                    hd = 2 * pr + i
                    c = dve.op(lambda e, hd=hd: e.scalar_tensor_tensor(
                        oT[:, hd, :], oT[:, hd, :], colv("ret_g", hd), gs[:, hd, :], ALU.mult, ALU.mult),
                        a, gs_tok[pr])
                    put_hi(hd, oT[:, hd, :], c)
                    if hd:
                        put_lo(hd - 1, oT[:, hd - 1, :])
            put_lo(3, oT[:, 3, :])
            product_out.finish()

        def conformer():
            UP = 32 + T
            u_r = Slots([scratch(i * UP, UP) for i in range(3)])
            o0 = 3 * UP
            t_ring = Slots([scratch(o0 + i * 512, 512) for i in range(2)])
            s_ring = Slots([scratch(o0 + 1024 + i * T, T) for i in range(2)])
            o1 = o0 + 1024 + 2 * T
            dw = scratch(o1, 8 * T).rearrange("p (a b) -> p a b", a=8)
            o2 = o1 + 8 * T
            acc2 = [scratch(o2 + i * T, T) for i in range(2)]
            o3 = o2 + 2 * T
            dsq = scratch(o3, 8 * T).rearrange("p (a b) -> p a b", a=8)
            o4 = o3 + 8 * T
            dgr = Slots([scratch(o4 + i * P, P) for i in range(DIAGS)])
            assert o4 + DIAGS * P <= SCR
            pads = [pool.op(lambda e, i=i: e.memset(u_r.aps[i][:, 0:32], 0.0), f_tok[KF - 1][1]) for i in range(3)]
            dw_tok = [None] * 8

            def evac(u, b, ps, tok):
                i, t, free = t_ring.next()
                j, s, sfree = s_ring.next()
                l, ub, ufree = u_r.next()
                u_r.free[l] = []
                a = dve.op(lambda e: e.tensor_tensor(t.rearrange("p (a b) -> p a b", a=2),
                                                     ps.rearrange("p (a b) -> p a b", a=2),
                                                     stretch(rbc[:, :], 1, 2), ALU.mult), tok, rs["t"], *free)
                free_bank(b, a)
                rs["used"] = [a]
                c = act.op(lambda e: e.activation(s, t[:, T:2 * T], ACT.Sigmoid, bias=colv("b_pw1", 8 + u)), a,
                           *sfree)
                if u >= 2:
                    mean(u - 2)
                if u >= 1:
                    taps(u - 1)
                    chains(u - 1)
                d = dve.op(lambda e: e.scalar_tensor_tensor(ub[:, 32:UP], t[:, 0:T], colv("b_pw1", u), s,
                                                            ALU.add, ALU.mult), c, pads[l], *ufree)
                t_ring.free[i] = s_ring.free[j] = [d]
                diags = []
                for k in range(TAPS[u]):
                    i, dgk, dfree = dgr.next()
                    x = act.op(lambda e, dgk=dgk, k=k: e.activation(dgk, ident, ACT.Copy, scale=colv("w_dw", 8 * k + u)),
                               cst_in, col_in, f_tok[KF - 1][1], *dfree)
                    diags.append((i, dgk, k, x))
                todo[u] = l, ub, d, diags

            def chains(u):
                l, ub, d, _ = todo[u]
                acc = [dw[:, u, :], acc2[u % 2]]
                ct = [None, None]
                for n, k in enumerate(range(TAPS[u], 31)):
                    q = n % 2
                    src = ub[:, 2 + k:2 + k + T]
                    wk = colv("w_dw", 8 * k + u)
                    if n == 0:
                        ct[0] = dve.op(lambda e, src=src, wk=wk: e.tensor_scalar(acc[0], src, wk, colv("b_dw", u), ALU.mult, ALU.add),
                                       d)
                    elif n == 1:
                        ct[1] = dve.op(lambda e, src=src, wk=wk: e.tensor_scalar(acc[1], src, wk, None, ALU.mult), d)
                    else:
                        ct[q] = dve.op(lambda e, q=q, src=src, wk=wk: e.scalar_tensor_tensor(acc[q], src, wk, acc[q], ALU.mult, ALU.add),
                                       ct[q])
                u_r.free[l] += [ct[0], ct[1]]
                a = dve.op(lambda e: e.tensor_tensor(acc[0], acc[0], acc[1], ALU.add), ct[0], ct[1])
                b, ps, tok = tap_bank[u]
                dw_tok[u] = dve.op(lambda e: e.tensor_tensor(dw[:, u, :], ps[:, 0:T], dw[:, u, :], ALU.add), tok, a)
                free_bank(b, dw_tok[u])

            todo, tap_bank = {}, {}
            mean_bank = []

            def taps(u):
                l, ub, d, diags = todo[u]
                b, ps = bank()
                for n, (i, dgk, k, x) in enumerate(diags):
                    tok = mm(ps[:, 0:T], dgk, ub[:, 2 + k:2 + k + T], n == 0, n == len(diags) - 1, inc=True, toks=(x, d))
                    dgr.free[i] = [tok]
                u_r.free[l].append(tok)
                tap_bank[u] = b, ps, tok

            def mean(u):
                if not mean_bank:
                    mean_bank.append(bank())
                return mm(mean_bank[0][1][:, 0:T], one[:, :], dw[:, u, :], u == 0, u == 7, inc=True,
                          toks=(dw_tok[u],))

            product(KD, [2] * KD, xh, xl, x_tok, evac, rms_hooks(10, 20))
            mean(6)
            taps(7)
            chains(7)
            tok = mean(7)
            b, ps = mean_bank[0]
            q_tok = []
            for i in range(4):
                a = dve.op(lambda e, i=i, ps=ps: e.scalar_tensor_tensor(
                    dw[:, 2 * i:2 * i + 2, :], stretch(ps[:, 0:T], 1, 2), -1.0 / D, dw[:, 2 * i:2 * i + 2, :],
                    ALU.mult, ALU.add), tok)
                q_tok.append(act.op(lambda e, i=i: e.activation(dsq[:, 2 * i:2 * i + 2, :], dw[:, 2 * i:2 * i + 2, :],
                                                                ACT.Square), a))
            free_bank(b, a)
            b, ps = bank()
            for j in range(4):
                for i in range(2):
                    tok = mm(ps[:, i:i + 1], dsq[:, j, i * P:(i + 1) * P], one[:, 0:1], j == 0 and i == 0, False,
                             toks=(q_tok[j // 2],), skip=True)
            a = dve.op(lambda e: e.tensor_tensor(dsq[:, 4:6, :], dsq[:, 4:6, :], dsq[:, 6:8, :], ALU.add), q_tok[2], q_tok[3])
            a = dve.op(lambda e: e.tensor_tensor(dsq[:, 4, :], dsq[:, 4, :], dsq[:, 5, :], ALU.add), a)
            for i in range(2):
                tok = mm(ps[:, i:i + 1], dsq[:, 4, i * P:(i + 1) * P], one[:, 0:1], False, True, inc=True, toks=(a,),
                         skip=True)
            sq_read = tok
            a = dve.op(lambda e, ps=ps: e.tensor_scalar(st[:, 0, :], ps[:, 0:2], 1.0 / D, EPS, ALU.mult, ALU.add), tok)
            free_bank(b, a)
            c = pool.op(lambda e: e.tensor_tensor(st[:, 1, :], st[:, 0, :], mh[:, 0:2], ALU.pow), a)
            for i in range(2):
                d = dve.op(lambda e, i=i: e.tensor_scalar(dg[:, i, :], ident, st[:, 1, i:i + 1], None, ALU.mult), c)
            b, ps = bank()
            tok = mm(ps[:, 0:T], one[:, :], dg[:, :, :].rearrange("p a b -> p (a b)"), True, True, inc=True,
                     toks=(d,))
            product_out = OutProduct(range(KD), N_CONF, gain_of("ffn_g", 8), bias="b_pw2")
            for i in range(4):
                a = dve.op(lambda e, i=i, ps=ps: e.tensor_tensor(
                    dw[:, 2 * i:2 * i + 2, :], stretch(ps[:, 0:T], 1, 2), dw[:, 2 * i:2 * i + 2, :], ALU.mult), tok,
                    q_tok[i])
                for j in (2 * i, 2 * i + 1):
                    s = act.op(lambda e, j=j: e.activation(dsq[:, j, :], dw[:, j, :], ACT.Silu,
                                                           scale=colv("ln_g", j), bias=colv("ln_b", j)), a, sq_read)
                    put_f(j, dsq[:, j, :], (s,))
                if i == 3:
                    free_bank(b, a)
                if i < 2:
                    product_out.outer(8 + 4 * i)
            product_out.finish()

        def short_conv():
            UP = 8 + T
            u_r = Slots([scratch(i * UP, UP) for i in range(2)])
            o0 = 2 * UP
            tb = Slots([scratch(o0 + i * T, T) for i in range(2)])
            tc = Slots([scratch(o0 + 2 * T + i * T, T) for i in range(2)])
            y_r = Slots([scratch(o0 + 4 * T + i * T, T) for i in range(2)])
            pads = [pool.op(lambda e, i=i: e.memset(u_r.aps[i][:, 0:8], 0.0), f_tok[KF - 1][1]) for i in range(2)]
            y_of = {}

            def evac(u, b, ps, tok):
                j = u // 2
                if u % 2 == 0:
                    i, t, free = tb.next()
                    l, ub, ufree = u_r.next()
                    m, y, yfree = y_r.next()
                    a = dve.op(lambda e, t=t: e.tensor_tensor(t, ps[:, 0:T], rb2[:, :], ALU.mult), tok, rs["t"], *free)
                    c = dve.op(lambda e, t=t: e.tensor_tensor(ub[:, 8:UP], ps[:, T:2 * T], t, ALU.mult), a, pads[l],
                               *ufree)
                    free_bank(b, c)
                    tb.free[i] = [c]
                    d = act.op(lambda e, y=y: e.activation(y, ub[:, 6:6 + T], ACT.Copy, scale=colv("w_c3", j)), c,
                               *yfree)

                    def taps():
                        f = dve.op(lambda e: e.scalar_tensor_tensor(y, ub[:, 7:7 + T], colv("w_c3", 8 + j), y,
                                                                    ALU.mult, ALU.add), d)
                        f = dve.op(lambda e: e.scalar_tensor_tensor(y, ub[:, 8:8 + T], colv("w_c3", 16 + j), y,
                                                                    ALU.mult, ALU.add), f)
                        u_r.free[l] = [f]
                        y_of[j] = (m, y, f)

                    later.append(taps)
                else:
                    if j not in y_of:
                        drain()
                    m, y, yt = y_of[j]
                    i, t, free = tc.next()
                    a = dve.op(lambda e, t=t: e.tensor_tensor(t, ps[:, 0:T], rbc[:, :], ALU.mult), tok, rs["t"], *free)
                    free_bank(b, a)
                    rs["used"] = [a]


                    def gate():
                        c = dve.op(lambda e: e.tensor_tensor(t, t, y, ALU.mult), a, yt)
                        y_r.free[m] = [c]
                        put_hi(j, t, c)

                    def rest():
                        tc.free[i] = [put_lo(j, t)]
                        res[j] = dve.op(lambda e: e.scalar_tensor_tensor(h[:, j, :], h[:, j, :], colv("fin_g", j),
                                                                         r1b, ALU.mult, ALU.mult),
                                        rs["r1b"], *rs["h_read"])

                    later.extend((gate, rest))

            res = {}
            r1b = scratch(SCR - T, T)

            def double_b():
                b, ps = bank()
                tok = mm(ps, one[:, :], dg4[:, :, :].rearrange("p a b -> p (a b)"), True, True, inc=True,
                         toks=(rs["dg"],))
                rs["r1b"] = dve.op(lambda e: e.tensor_copy(r1b, ps[:, 0:T]), tok)
                t = dve.op(lambda e: e.tensor_copy(rbc[:, :], ps[:, T:2 * T]), *rs["used"])
                rs["used"] = []
                free_bank(b, t)
                rs["t"] = dve.op(lambda e: e.tensor_tensor(rb2[:, :], rbc[:, :], rbc[:, :], ALU.mult), t)
                return True

            product(KD, [2, 1] * KD, xh, xl, x_tok, evac, {24: double_a, 48: double_b})
            OutProduct(range(KD), N_SHORT, gain_of("ffn2_g", 0)).finish()

        def attention():
            o = [0]

            def take(n):
                o[0] += n
                return scr[:, o[0] - n:o[0]]

            qn = take(2 * D).rearrange("p (a b) -> p a b", a=2)
            kv = take(1024).rearrange("p (a b) -> p a b", a=2)
            kd = take(1024).rearrange("p (a b) -> p a b", a=2)
            qT = take(8 * T).rearrange("p (a b) -> p a b", a=8)
            kT = take(4 * T).rearrange("p (a b) -> p a b", a=4)
            sc = [take(2 * 386).rearrange("p (a b) -> p a b", a=2) for _ in range(2)]
            sc.append(kd.rearrange("p a b -> p (a b)")[:, 0:772].rearrange("p (a b) -> p a b", a=2))
            pT = [take(768).rearrange("p (a b) -> p a b", a=2) for _ in range(2)]
            small = [take(8) for _ in range(3)]
            qg = take(1)
            r1 = take(32)
            r2 = take(32)
            start = f_tok[KF - 1][1]
            qg_t = dve.op(lambda e: e.tensor_scalar(qg, colv("q_g", 0), 0.125, None, ALU.mult), col_in, start)

            def project(middle=None):
                bs = [bank(), bank()]
                for k in range(KD):
                    if middle and k in middle:
                        middle[k]()
                    wt = Stream.take(4)
                    for i in range(2):
                        tok = mm3(bs[i][1], wt, xh[:, k, i * P:(i + 1) * P], xl[:, k, i * P:(i + 1) * P], x_tok[k],
                                  k == 0, k == KD - 1, False, end=(i == 1 and wt[3]))
                return bs, tok

            def heads(ap):
                return ap.rearrange("p (a b) -> p a b", b=64)

            def head_norm(src, n, tok, r, sqb, dst):
                a = act.op(lambda e: e.activation(sqb, src, ACT.Square), *tok)

                def power():
                    c = dve.op(lambda e: e.tensor_reduce(r[:, 0:n], sqb, AX.X, ALU.add), a)
                    d = dve.op(lambda e: e.tensor_scalar(r[:, 0:n], r[:, 0:n], 1.0 / 64, EPS, ALU.mult, ALU.add), c)
                    f = pool.op(lambda e: e.tensor_tensor(r[:, n:2 * n], r[:, 0:n], mh[:, 0:n], ALU.pow), d)

                    def scale():
                        for out_ in dst:
                            g = dve.op(lambda e, out_=out_: e.tensor_tensor(out_, src, stretch(r[:, n:2 * n], 2, 64),
                                                                            ALU.mult), f)
                        return g
                    return scale
                return power

            sqb = [take(512) for _ in range(2)]
            assert o[0] <= SCR, o[0]
            kd_t, kT_t, qT_t, q_done = [], [], [], {}

            def k_transposes():
                for half in range(2):
                    b, ps = bank()
                    for g in range(2):
                        for i in range(2):
                            gg = 2 * half + g
                            tok = pe.op(lambda e, g=g, gg=gg, i=i, ps=ps: e.transpose(
                                ps[:, (2 * g + i) * P:(2 * g + i + 1) * P], kd[:, i, gg * P:(gg + 1) * P], ident),
                                *kd_t)
                    a = act.op(lambda e, half=half, ps=ps: e.activation(
                        kT[:, 2 * half:2 * half + 2, :], ps.rearrange("p (a b) -> p a b", a=2), ACT.Copy,
                        scale=colv("k_g", 0)), tok)
                    free_bank(b, a)
                    kT_t.append(a)

            def q_transposes(t):
                b, ps = bank()
                for g in range(2):
                    for i in range(2):
                        tt = 2 * t + g
                        tok = pe.op(lambda e, g=g, i=i, tt=tt: e.transpose(
                            ps[:, (2 * g + i) * P:(2 * g + i + 1) * P], qn[:, i, tt * P:(tt + 1) * P], ident),
                            q_done[t // 2, i])
                a = act.op(lambda e: e.activation(
                    qT[:, 2 * t:2 * t + 2, :], ps.rearrange("p (a b) -> p a b", a=2), ACT.Copy, scale=qg), tok, qg_t)
                free_bank(b, a)
                qT_t.append(a)

            def q_scale(c, qb, q_mm):
                toks = []
                for i in range(2):
                    dst = qn[:, i, c * 512:(c + 1) * 512]
                    a = dve.op(lambda e, dst=dst, i=i: e.tensor_scalar(dst, qb[i][1], st[:, 1, i:i + 1], None, ALU.mult), q_mm, rs["pow"])
                    free_bank(qb[i][0], a)
                    toks.append(a)
                return toks

            def q_norm(c, i, tok):
                sq_free = (kd_t[i],) if c else ()
                src = heads(qn[:, i, c * 512:(c + 1) * 512])
                return head_norm(src, 8, (tok, *sq_free), r2[:, 16 * i:16 * i + 16], heads(sqb[i]), [src])

            q0b, q0_mm = project()
            rms_a(diagonals=False)
            q0 = q_scale(0, q0b, q0_mm)
            steps = [q_norm(0, i, q0[i]) for i in range(2)]
            steps = [power() for power in steps]
            for i in range(2):
                q_done[0, i] = steps[i]()
            kvb, kv_mm = project()
            kvt = []
            for i in range(2):
                a = dve.op(lambda e, i=i: e.tensor_scalar(kv[:, i, :], kvb[i][1], st[:, 1, i:i + 1], None, ALU.mult),
                           kv_mm, rs["pow"])
                free_bank(kvb[i][0], a)
                kvt.append(a)

            steps = []
            for i in range(2):
                twice = [kd[:, i, 0:512].rearrange("p (g j d) -> p g j d", j=2, d=64)[:, :, j, :] for j in range(2)]
                steps.append(head_norm(heads(kv[:, i, 0:256]), 4, (kvt[i], q_done[0, i]), r1[:, 8 * i:8 * i + 8],
                                      heads(sqb[i][:, 0:256]), twice))
            steps = [power() for power in steps]
            kd_t += [scale() for scale in steps]

            negd = cst[:, C_NEG:C_NEG + 384]
            sunk, exps, normed, pTt, val_bank = {}, {}, {}, {}, {}
            sc_free, pT_free, small_free = [[], [], kT_t], [[], []], [[], [], []]

            def put_sinks(p):
                s = sc[p % 3]
                both = row[:, 2 * p:2 * p + 2]
                sunk[p] = pool.op(lambda e: e.tensor_copy(s[:, :, 0:386:385], stretch(both, 2, 2)), row_in, start,
                                  *sc_free[p % 3])

            sc_bank = {}

            def scores(p):
                g = p // 2
                bs = [bank(), bank()]
                for part in range(2):
                    for odd in range(2):
                        r = slice(64 * odd, 64 * odd + 64)
                        ps = bs[odd][1]
                        dst, q_ap = (ps[:, 0:P], qT[r, p, 0:P]) if part == 0 else (ps[:, P:3 * P], qT[r, p, P:T])
                        k_ap = kT[r, g, 0:P] if part == 0 else kT[r, g, :]
                        tok = mm(dst, q_ap, k_ap, True, True, inc=True, toks=(qT_t[p // 2], kT_t[g // 2]))
                sc_bank[p] = bs, tok

            def softmax(p):
                s = sc[p % 3]
                bs, tok = sc_bank[p]
                for odd in range(2):
                    slope = float(2.0 ** (-8.0 * (2 * p + odd + 1) / 16))
                    ps = bs[odd][1]
                    a = dve.op(lambda e, odd=odd, ps=ps, slope=slope: e.scalar_tensor_tensor(s[:, odd, 1:385], negd, slope, ps[:, 0:384],
                                                                ALU.mult, ALU.add), tok, start, *sc_free[p % 3])
                    free_bank(bs[odd][0], a)
                nm, den = small[p % 3][:, 0:4], small[p % 3][:, 4:8]
                m0 = dve.op(lambda e: e.tensor_reduce(nm[:, 0:2], s[:, :, 0:129], AX.X, ALU.max), a, sunk[p],
                            *small_free[p % 3])
                m1 = dve.op(lambda e: e.tensor_reduce(nm[:, 2:4], s[:, :, 129:386], AX.X, ALU.max), a)
                m = dve.op(lambda e: e.tensor_scalar(nm, nm, -1.0, None, ALU.mult), m0, m1)
                for c in range(4):
                    part, odd = c // 2, c % 2
                    span = s[:, odd, 0:129] if part == 0 else s[:, odd, 129:386]
                    x = act.op(lambda e, c=c, span=span: e.activation(span, span, ACT.Exp, bias=nm[:, c:c + 1],
                                                      accum_out=den[:, c:c + 1]), m)
                exps[p] = x

            def divide(p):
                s = sc[p % 3]
                den = small[p % 3][:, 4:8]
                a = dve.op(lambda e: e.reciprocal(den, den), exps[p])
                for c in range(4):
                    part, odd = c // 2, c % 2
                    span = s[:, odd, 1:129] if part == 0 else s[:, odd, 129:385]
                    x = dve.op(lambda e, c=c, span=span: e.tensor_scalar(span, span, den[:, c:c + 1], None, ALU.mult), a)
                small_free[p % 3] = [x]
                normed[p] = x

            def weigh(p):
                s = sc[p % 3]
                toks = []
                for odd in range(2):
                    b, ps = bank()
                    for part in range(3):
                        src = s[:, odd, 1 + part * P:1 + (part + 1) * P]
                        tok = pe.op(lambda e, part=part, ps=ps, src=src: e.transpose(ps[:, part * P:(part + 1) * P], src, ident), normed[p],
                                    cst_in)
                    dst = pT[p % 2][:, odd, :]
                    if odd:
                        a = dve.op(lambda e, dst=dst, ps=ps: e.tensor_copy(dst, ps[:, 0:384]), tok, *pT_free[p % 2])
                    else:
                        a = act.op(lambda e, dst=dst, ps=ps: e.activation(dst, ps[:, 0:384], ACT.Copy), tok, *pT_free[p % 2])
                    free_bank(b, a)
                    toks.append(a)
                sc_free[p % 3] = [tok]
                pTt[p] = toks

            def values(p):
                g = p // 2
                vs = [kv[:, m_, 256 + 64 * g:256 + 64 * g + 64] for m_ in range(2)]
                b, ps = bank()
                pr = [pT[p % 2][:, :, k * P:(k + 1) * P] for k in range(3)]
                two = [ps[0:64, k * T:(k + 1) * T].rearrange("p (a b) -> p a b", a=2) for k in range(2)]
                mm(two[0], vs[0], pr[0], True, True, toks=(*pTt[p], *kvt))
                mm(two[1], vs[0], pr[1], True, False)
                tok = mm(two[1], vs[1], pr[2], False, True, inc=True)
                pT_free[p % 2] = [tok]
                val_bank[p] = b, ps, tok

            def outputs_hi(p):
                b, ps, tok = val_bank[p]
                by_head = ps[0:64, :].rearrange("p (a h b) -> p a h b", a=2, h=2)
                val_bank[p] = b, by_head
                for odd in range(2):
                    r = slice(64 * odd, 64 * odd + 64)
                    dst = fh[r, p, :].rearrange("p (a b) -> p a b", a=2)
                    a = act.op(lambda e, dst=dst, odd=odd: e.activation(dst, by_head[:, :, odd, :], ACT.Copy), tok)
                f_tok[p] = (a, None)

            def outputs_lo(p):
                b, by_head = val_bank[p]
                a = f_tok[p][0]
                for odd in range(2):
                    r = slice(64 * odd, 64 * odd + 64)
                    hi = fh[r, p, :].bitcast(F32).rearrange("p (a b) -> p a b", a=2)
                    dst = fl[r, p, :].rearrange("p (a b) -> p a b", a=2)
                    c = dve.op(lambda e, dst=dst, hi=hi, odd=odd: e.tensor_tensor(dst, by_head[:, :, odd, :], hi, ALU.subtract), a)
                free_bank(b, c)
                f_tok[p] = (a, c)

            product_out = OutProduct(range(KD), N_ATT, gain_of("ffn2_g", 8))
            q1 = []

            def first_scores():
                scores(0)

            def first_softmax():
                scores(1)
                softmax(0)
                softmax(1)

            put_sinks(0)
            put_sinks(1)
            q1b, q1_mm = project({2: lambda: q_transposes(0), 3: lambda: q_transposes(1), 4: k_transposes, 5: first_scores, 6: first_softmax})
            put_sinks(2)
            divide(0)
            q1 = q_scale(1, q1b, q1_mm)
            rs["st"] = [q1[1]]
            weigh(0)
            steps = [q_norm(1, i, q1[i]) for i in range(2)]
            for p in range(8):
                if p:
                    weigh(p)
                if p < 6:
                    scores(p + 2)
                if p < 5:
                    put_sinks(p + 3)
                if p >= 2:
                    product_out.outer(4)
                values(p)
                outputs_hi(p)
                if p < 7:
                    divide(p + 1)
                if p == 0:
                    steps = [power() for power in steps]
                if p == 1:
                    for i in range(2):
                        q_done[1, i] = steps[i]()
                    q_transposes(2)
                if p == 2:
                    q_transposes(3)
                if p < 6:
                    softmax(p + 2)
                if p >= 2:
                    product_out.outer(4)
                outputs_lo(p)
            product_out.finish()

        keep_warm(WARM_START)
        load_chunk(1)
        cst_in = load(sp, "cst", cst[:, :], consts)
        load_chunk(2)
        pw_in = load(sp, "pw", pw[:, :, :], poolw)
        row_in = load(sp, "row", row[:, :], rows)
        for k in range(KD):
            prep(k, gain_of("mix_g", 0), (x_in[0 if k < 2 else 1], col0_in), None)
            if k in (1, 7):
                split_hi(k // 4)
                split_lo(k // 4)
        for p in range(2, RING - 1):
            if p == 2:
                for _ in range(4):
                    angle_steps.pop(0)()
            if p == RING - 2:
                while sums_due:
                    sums_due.pop(0)()
                    angle_steps.pop(0)()
            split_hi(p)
            split_lo(p)
        gg_tok = dve.op(lambda e: e.tensor_tensor(gg[:, :], col[:, COLS["fin_g"]:COLS["fin_g"] + KD],
                                                  col[:, COLS["mix2_g"]:COLS["mix2_g"] + KD], ALU.mult), col_in)
        act.wait(gg_tok)
        later.extend((lambda: None, lambda: None, lambda: None, retention_sines))
        retention()
        ffn(gain_of("mix_g", 8))
        conformer()
        ffn(lambda k: gg[:, k:k + 1], squares=gain_of("fin_g", 0))
        short_conv()
        ffn(gain_of("mix2_g", 8))
        attention()
        ffn(None)
        sp.wait((s_out, 16 * KD))
        assert Stream.g == 8 * n_pieces

        block = ctx.enter_context(nc.Block())

        @block.sync
        def _(e):
            sp.play(e)

        @block.gpsimd
        def _(e):
            pool.play(e)

        @block.scalar
        def _(e):
            act.play(e)

        @block.vector
        def _(e):
            dve.play(e)

        @block.tensor
        def _(e):
            pe.play(e)


def kernel(**inputs):
    import numpy as _np
    import concourse.bacc as _bacc
    from concourse import mybir as _mybir
    from concourse.bass_utils import run_bass_kernel_spmd as _run

    a = {k: _np.asarray(v) for k, v in inputs.items()}

    def tiles(w):
        k, n = w.shape
        return w.reshape(k // 128, 128, n // 128, 128).transpose(1, 2, 0, 3)

    def strips(w):
        k, n = w.shape
        return w.reshape(k // 128, 128, n // 512, 512).transpose(1, 2, 0, 3)

    def flat(t):
        return t.reshape(128, -1)

    def wide(t, n):
        return _np.concatenate([flat(t[:, 0:n].transpose(0, 2, 1, 3)), flat(t[:, n:])], axis=1)

    def outer(w, order, n):
        t = tiles(w)[:, :, list(order), :]
        return _np.concatenate([flat(t[:, :, 0:n].transpose(0, 2, 1, 3)), flat(t[:, :, n:])], axis=1)

    def mixed(*parts):
        t = _np.stack(parts, axis=2)
        return t.reshape(128, -1, *t.shape[3:])

    w_in = a["ret_w_in"][0]
    c_in = a["conv_w_in_2"][0]
    qkv = a["attn_w_qkv_2"][0]
    pw1 = a["conv_w_pw1"][0]
    gu2 = a["ffn_w_gate_up_2"]

    def ffn(gate, up, down):
        return [wide(mixed(tiles(gate), tiles(up)), 2 * WIDE), flat(tiles(down))]

    parts = [flat(tiles(w_in[:, 0:1024])), flat(strips(w_in[:, 1024:1536])), flat(tiles(w_in[:, 2048:2560])),
             flat(tiles(w_in[:, 1536:2048])), outer(a["mix_w_out"][0], (4, 5, 6, 7, 0, 1, 2, 3), N_RET)]
    parts += ffn(a["ffn_w_gate"][0], a["ffn_w_up"][0], a["ffn_w_down"][0])
    parts += [flat(mixed(tiles(pw1[:, 0:1024]), tiles(pw1[:, 1024:2048]))), outer(a["conv_w_pw2"][0], range(8), N_CONF)]
    parts += ffn(a["ffn_w_gate"][1], a["ffn_w_up"][1], a["ffn_w_down"][1])
    parts += [flat(mixed(tiles(c_in[:, 0:1024]), tiles(c_in[:, 2048:3072]), tiles(c_in[:, 1024:2048]))),
              outer(a["conv_w_out_2"][0], range(8), N_SHORT)]
    parts += ffn(gu2[0][:, 0:2816], gu2[0][:, 2816:], a["ffn_w_down_2"][0])
    parts += [flat(strips(qkv[:, 0:512])), flat(strips(qkv[:, 1024:1536])), flat(strips(qkv[:, 512:1024])), outer(a["attn_w_o_2"][0], range(8), N_ATT)]
    parts += ffn(gu2[1][:, 0:2816], gu2[1][:, 2816:], a["ffn_w_down_2"][1])
    w = _np.concatenate(parts, axis=1)
    w = _np.ascontiguousarray(w.reshape(128, -1, CHUNK).transpose(1, 0, 2))

    def column(v):
        return _np.asarray(v).reshape(-1, 128).T

    f = _np.float32(10000.0) ** (-_np.arange(64, dtype=_np.float32) / _np.float32(64))
    inv = _np.concatenate([f, f])[:, None]
    sgn = _np.where(_np.arange(128) < 64, -1.0, 1.0).astype(_np.float32)[:, None]
    cols = _np.ascontiguousarray(_np.concatenate([
        column(a["mixer_norm_g"]), inv, sgn, column(a["ffn_norm_g"]), column(a["final_norm_g"]), column(a["ret_norm_g"]),
        column(a["pool_scale"]), column(a["conv_b_pw1"]), column(a["conv_w_dw"][0]), column(a["conv_b_dw"]),
        column(a["conv_ln_g"]), column(a["conv_ln_b"]), column(a["conv_b_pw2"]), column(a["conv_w_2"][0]),
        column(a["norm_mixer_2"]), column(a["norm_ffn_2"]),
        _np.tile(a["attn_q_gain_2"].T, (2, 1)), _np.tile(a["attn_k_gain_2"].T, (2, 1))], axis=1))
    rows = _np.ascontiguousarray(_np.broadcast_to(a["attn_sinks_2"], (128, NROW)))
    pos = _np.ascontiguousarray(_np.broadcast_to(a["positions"].reshape(1, 256), (128, 256)))
    xT = _np.ascontiguousarray(a["x"][0].T.reshape(8, 128, 256).transpose(1, 0, 2))
    poolw = _np.ascontiguousarray(a["pool_w"][0].transpose(1, 0, 2))

    c = _np.zeros((128, NCONST), _np.float32)
    c[:, C_ID:C_ID + 128] = _np.eye(128)
    i = _np.arange(128)[:, None]
    j = _np.arange(256)[None, :]
    for hd in range(4):
        lg = _np.log1p(-(2.0 ** (-5.0 - hd)))
        c[:, C_DEC + 256 * hd:C_DEC + 256 * hd + 256] = _np.where(
            j >= i, _np.exp(lg * _np.maximum(j - i, 0)), 0.0) * 128.0 ** -0.5
    dist = i + 128 - j
    far = _np.where((dist >= 0) & (dist < 128), -dist, -1e33)
    c[:, C_NEG:C_NEG + 384] = _np.concatenate([far[:, 128:256], far], axis=1)
    for g in range(4):
        wnd = 2 << g
        c[:, C_COR + 16 * g:C_COR + 16 * g + 16] = wnd / _np.minimum(_np.arange(16) + 1, wnd)

    nc = _bacc.Bacc("TRN2", target_bir_lowering=False, num_devices=1)
    arrays = {"w": w, "poolw": poolw, "xT": xT, "pos": pos, "cols": cols, "rows": rows, "consts": c}
    aps = [nc.dram_tensor(n, v.shape, _mybir.dt.from_np(v.dtype), kind="ExternalInput").ap()
           for n, v in arrays.items()]
    out = nc.dram_tensor("out", (128, 8, 256), _mybir.dt.float32, kind="ExternalOutput").ap()
    model_kernel(nc, *aps, out)
    r = _run(nc, [arrays], core_ids=[0])
    got = _np.asarray(r.results[0]["out"])
    return _np.ascontiguousarray(got.transpose(1, 0, 2).reshape(1024, 256).T)[None]
```
